# Optimizing a Trainium2 kernel written in Bass

```python
import math
import jax, jax.numpy as jnp
from jax import lax
import numpy as np

D_MODEL = 1024
BATCH = 1
SEQ = 256
DEPTH = 1

CHUNK = 64
Q_BLOCK = 128
N_MEM = 256
MIX_WIDTH = D_MODEL
FOX_WIDTH = MIX_WIDTH // 2
HGRN_WIDTH = MIX_WIDTH - FOX_WIDTH
FOX_HEAD_DIM = 64
FOX_HEADS = FOX_WIDTH // FOX_HEAD_DIM
HGRN_KEY_DIM = 128
HGRN_HEADS = HGRN_WIDTH // HGRN_KEY_DIM
HGRN_VAL_DIM = HGRN_WIDTH // HGRN_HEADS
X_HEADS = 4
X_HEAD_DIM = D_MODEL // X_HEADS
D_FF = 4 * D_MODEL
EPS = 1e-6
SPLITS = (FOX_WIDTH, FOX_WIDTH, FOX_WIDTH, FOX_HEADS, HGRN_WIDTH, HGRN_WIDTH, HGRN_WIDTH, HGRN_WIDTH)
IN_COLS = sum(SPLITS)


def rmsnorm(x, g):
    xf = x.astype(jnp.float32)
    y = xf * lax.rsqrt(jnp.mean(xf * xf, axis=-1, keepdims=True) + EPS)
    return (y * g.astype(jnp.float32)).astype(x.dtype)

def fox_attention(q, k, v, log_f):
    b_, h_, s_, d_ = q.shape
    nb = s_ // Q_BLOCK
    scale = 1.0 / math.sqrt(d_)
    F = jnp.cumsum(log_f, axis=-1)
    qb = q.reshape(b_, h_, nb, Q_BLOCK, d_).transpose(2, 0, 1, 3, 4)
    Fb = F.reshape(b_, h_, nb, Q_BLOCK).transpose(2, 0, 1, 3)
    pos = jnp.arange(s_, dtype=jnp.int32).reshape(nb, Q_BLOCK)
    key_pos = jnp.arange(s_, dtype=jnp.int32)

    def block(args):
        qi, Fi, pi = args
        s = jnp.einsum('bhqd,bhkd->bhqk', qi, k).astype(jnp.float32) * scale
        s = s + Fi[..., None] - F[:, :, None, :]
        mask = pi[:, None] >= key_pos[None, :]
        s = jnp.where(mask, s, -jnp.inf)
        p = jax.nn.softmax(s, axis=-1)
        return jnp.einsum('bhqk,bhkd->bhqd', p.astype(v.dtype), v)

    out = lax.map(block, (qb, Fb, pos))
    return out.transpose(1, 2, 0, 3, 4).reshape(b_, h_, s_, d_)

def hgrn2_chunkwise(q, f_logit, i, lb):
    b_, s_, _ = q.shape
    n_c = s_ // CHUNK

    def heads(t, d):
        return t.astype(jnp.float32).reshape(b_, n_c, CHUNK, HGRN_HEADS, d).transpose(1, 0, 3, 2, 4)

    lbh = lb.astype(jnp.float32).reshape(HGRN_HEADS, 1, HGRN_KEY_DIM)
    f = lbh + (1.0 - lbh) * jax.nn.sigmoid(heads(f_logit, HGRN_KEY_DIM))
    kk = 1.0 - f
    g = jnp.log(f)
    qq = jax.nn.silu(heads(q, HGRN_KEY_DIM))
    ii = heads(i, HGRN_VAL_DIM)
    causal = jnp.tril(jnp.ones((CHUNK, CHUNK), dtype=bool))

    def step(state, inp):
        qc, kc, ic, gc = inp
        bcum = jnp.cumsum(gc, axis=2)
        diff = bcum[:, :, :, None, :] - bcum[:, :, None, :, :]
        decay = jnp.exp(jnp.where(causal[:, :, None], diff, -jnp.inf))
        attn = jnp.einsum('bhtd,bhsd,bhtsd->bhts', qc, kc, decay)
        intra = jnp.einsum('bhts,bhsv->bhtv', attn, ic)
        inter = jnp.einsum('bhtd,bhdv->bhtv', qc * jnp.exp(bcum), state)
        b_last = bcum[:, :, -1]
        k_dec = kc * jnp.exp(b_last[:, :, None, :] - bcum)
        new_state = jnp.exp(b_last)[..., None] * state + jnp.einsum('bhsd,bhsv->bhdv', k_dec, ic)
        return new_state, intra + inter

    s0 = jnp.zeros((b_, HGRN_HEADS, HGRN_KEY_DIM, HGRN_VAL_DIM), jnp.float32)
    _, outs = lax.scan(step, s0, (qq, kk, ii, g))
    return outs.transpose(1, 0, 3, 2, 4).reshape(b_, s_, HGRN_HEADS, HGRN_VAL_DIM)

def memory_cross_attention(h, mem_n, w_q, w_kv, w_o):
    b_, s_, _ = h.shape
    m_ = mem_n.shape[1]
    q = (h @ w_q).reshape(b_, s_, X_HEADS, X_HEAD_DIM)
    kv = mem_n @ w_kv
    k, v = jnp.split(kv, 2, axis=-1)
    k = k.reshape(b_, m_, X_HEADS, X_HEAD_DIM)
    v = v.reshape(b_, m_, X_HEADS, X_HEAD_DIM)
    s = jnp.einsum('bshd,bmhd->bhsm', q, k).astype(jnp.float32) / math.sqrt(X_HEAD_DIM)
    p = jax.nn.softmax(s, axis=-1)
    o = jnp.einsum('bhsm,bmhd->bshd', p.astype(v.dtype), v).reshape(b_, s_, D_MODEL)
    return o @ w_o

def first_inputs(seed: int = 0) -> dict:
    key = jax.random.key(seed)
    ks = jax.random.split(key, 20)
    nrm = lambda k, shape, s: jax.random.normal(k, shape, jnp.float32) * s
    gain = lambda k, shape: 1.0 + 0.02 * jax.random.normal(k, shape, jnp.float32)
    return {
        "x": nrm(ks[0], (BATCH, SEQ, D_MODEL), 1.0),
        "mem": nrm(ks[1], (BATCH, N_MEM, D_MODEL), 1.0),
        "norm_mix_g": gain(ks[2], (DEPTH, D_MODEL)),
        "w_in": nrm(ks[3], (DEPTH, D_MODEL, IN_COLS), D_MODEL ** -0.5),
        "fox_f_bias": 1.0 + 0.1 * jax.random.normal(ks[4], (DEPTH, FOX_HEADS), jnp.float32),
        "hgrn_lb_logits": nrm(ks[5], (DEPTH + 1, HGRN_WIDTH), 0.1),
        "hgrn_norm_g": gain(ks[6], (DEPTH, HGRN_VAL_DIM)),
        "w_out": nrm(ks[7], (DEPTH, MIX_WIDTH, D_MODEL), MIX_WIDTH ** -0.5),
        "norm_x_g": gain(ks[8], (DEPTH, D_MODEL)),
        "norm_mem_g": gain(ks[9], (DEPTH, D_MODEL)),
        "w_xq": nrm(ks[10], (DEPTH, D_MODEL, D_MODEL), D_MODEL ** -0.5),
        "w_xkv": nrm(ks[11], (DEPTH, D_MODEL, 2 * D_MODEL), D_MODEL ** -0.5),
        "w_xo": nrm(ks[12], (DEPTH, D_MODEL, D_MODEL), D_MODEL ** -0.5),
        "norm_ff_g": gain(ks[13], (DEPTH, D_MODEL)),
        "w1": nrm(ks[14], (DEPTH, D_MODEL, D_FF), D_MODEL ** -0.5),
        "w2": nrm(ks[15], (DEPTH, D_FF, D_MODEL), D_FF ** -0.5),
        "final_norm_g": gain(ks[16], (D_MODEL,)),
    }

def first_block(x, mem, norm_mix_g, w_in, fox_f_bias, hgrn_lb_logits, hgrn_norm_g, w_out,
              norm_x_g, norm_mem_g, w_xq, w_xkv, w_xo, norm_ff_g, w1, w2, final_norm_g):
    b_, s_, _ = x.shape
    lbs = jnp.cumsum(jax.nn.softmax(hgrn_lb_logits.astype(jnp.float32), axis=0), axis=0)
    split_idx = list(np.cumsum(SPLITS)[:-1])
    h = x
    for l in range(DEPTH):
        hn = rmsnorm(h, norm_mix_g[l])
        proj = hn @ w_in[l]
        fq, fk, fv, ff, gq, gf, gi, gg = jnp.split(proj, split_idx, axis=-1)
        to_heads = lambda t: t.reshape(b_, s_, FOX_HEADS, FOX_HEAD_DIM).transpose(0, 2, 1, 3)
        log_f = jax.nn.log_sigmoid((ff + fox_f_bias[l]).astype(jnp.float32)).transpose(0, 2, 1)
        fox_out = fox_attention(to_heads(fq), to_heads(fk), to_heads(fv), log_f)
        fox_out = fox_out.transpose(0, 2, 1, 3).reshape(b_, s_, FOX_WIDTH)
        rec = hgrn2_chunkwise(gq, gf, gi, lbs[l])
        rec = rmsnorm(rec, hgrn_norm_g[l]) * jax.nn.silu(
            gg.astype(jnp.float32).reshape(b_, s_, HGRN_HEADS, HGRN_VAL_DIM))
        rec = rec.reshape(b_, s_, HGRN_WIDTH).astype(h.dtype)
        h = h + jnp.concatenate([fox_out, rec], axis=-1) @ w_out[l]
        mem_n = rmsnorm(mem, norm_mem_g[l])
        h = h + memory_cross_attention(rmsnorm(h, norm_x_g[l]), mem_n, w_xq[l], w_xkv[l], w_xo[l])
        u = rmsnorm(h, norm_ff_g[l]) @ w1[l]
        h = h + jnp.square(jax.nn.relu(u)) @ w2[l]
    return rmsnorm(h, final_norm_g)


MEM_TOKENS = 256
N_MEM_HEADS = 4
DH_MEM = 128
MEM_WIDTH = N_MEM_HEADS * DH_MEM
N_DIFF_HEADS = 8
DH_DIFF = 64
DIFF_Q_WIDTH = N_DIFF_HEADS * 2 * DH_DIFF
DIFF_V_WIDTH = N_DIFF_HEADS * 2 * DH_DIFF
POOL_WINDOWS = (2, 4, 8, 16)
POOL_GROUPS = len(POOL_WINDOWS)
POOL_GROUP_WIDTH = 128
POOL_WIDTH = POOL_GROUPS * POOL_GROUP_WIDTH
N_BRANCHES = 3
IN_COLS_2 = 2 * DIFF_Q_WIDTH + DIFF_V_WIDTH + POOL_WIDTH + MEM_WIDTH + N_BRANCHES * D_MODEL
D_FF_2 = 2816
CONV_WIDTH = 3
NORM_EPS = 1e-6


def rms_norm(x, g):
    xf = x.astype(jnp.float32)
    y = xf * lax.rsqrt(jnp.mean(xf * xf, axis=-1, keepdims=True) + NORM_EPS)
    return (y * g.astype(jnp.float32)).astype(x.dtype)

def alibi_slopes(n_heads):
    return jnp.exp2(-8.0 * jnp.arange(1, n_heads + 1, dtype=jnp.float32) / n_heads)

def lambda_init_for(layer_idx):
    return 0.8 - 0.6 * math.exp(-0.3 * layer_idx)

def diff_attention(q, k, v, lam):
    B, S = q.shape[0], q.shape[1]
    n_blocks = S // Q_BLOCK
    scale = DH_DIFF ** -0.5
    slopes = alibi_slopes(N_DIFF_HEADS)
    kf = k.astype(jnp.float32)
    vf = v.astype(jnp.float32)
    kpos = jnp.arange(S)
    qb = q.astype(jnp.float32).reshape(B, n_blocks, Q_BLOCK, N_DIFF_HEADS, 2, DH_DIFF)
    qb = jnp.moveaxis(qb, 1, 0)

    def one_block(args):
        qblk, i = args
        qpos = i * Q_BLOCK + jnp.arange(Q_BLOCK)
        s = jnp.einsum('bqhcd,bkhcd->bhcqk', qblk, kf) * scale
        dist = qpos[:, None] - kpos[None, :]
        bias = -slopes[:, None, None] * dist.astype(jnp.float32)
        s = s + bias[None, :, None]
        s = jnp.where((dist >= 0)[None, None, None], s, jnp.finfo(jnp.float32).min)
        p = jax.nn.softmax(s, axis=-1)
        a = p[:, :, 0] - lam * p[:, :, 1]
        return jnp.einsum('bhqk,bkhe->bqhe', a, vf)

    out = lax.map(one_block, (qb, jnp.arange(n_blocks)))
    return jnp.moveaxis(out, 0, 1).reshape(B, S, N_DIFF_HEADS, 2 * DH_DIFF)

def multiscale_pool(u, pool_w, pool_scale):
    B, S, _ = u.shape
    uf = u.astype(jnp.float32).reshape(B, S, POOL_GROUPS, POOL_GROUP_WIDTH)
    csum = jnp.cumsum(uf, axis=1)
    cpad = jnp.concatenate([jnp.zeros_like(csum[:, :1]), csum], axis=1)
    t = jnp.arange(S)
    outs = []
    for g, w in enumerate(POOL_WINDOWS):
        lo = jnp.maximum(t + 1 - w, 0)
        window_sum = csum[:, :, g] - cpad[:, lo, g]
        count = jnp.minimum(t + 1, w).astype(jnp.float32)
        outs.append(window_sum / count[None, :, None] - uf[:, :, g])
    p = jnp.stack(outs, axis=2)
    y = jnp.einsum('bsgc,gcd->bsgd', p, pool_w.astype(jnp.float32))
    return (y.reshape(B, S, POOL_WIDTH) * pool_scale.astype(jnp.float32)).astype(u.dtype)

def memory_cross_attention_2(q, mem_n, w_mem_kv):
    B, S, _ = q.shape
    kv = mem_n @ w_mem_kv
    k_m, v_m = jnp.split(kv, 2, axis=-1)
    qh = q.astype(jnp.float32).reshape(B, S, N_MEM_HEADS, DH_MEM)
    kh = k_m.astype(jnp.float32).reshape(B, -1, N_MEM_HEADS, DH_MEM)
    vh = v_m.astype(jnp.float32).reshape(B, -1, N_MEM_HEADS, DH_MEM)
    s = jnp.einsum('bshd,bmhd->bhsm', qh, kh) * (DH_MEM ** -0.5)
    p = jax.nn.softmax(s, axis=-1)
    o = jnp.einsum('bhsm,bmhd->bshd', p, vh)
    return o.reshape(B, S, MEM_WIDTH).astype(q.dtype)

def causal_depthwise_conv(u, w, b):
    S = u.shape[1]
    up = jnp.pad(u, ((0, 0), (CONV_WIDTH - 1, 0), (0, 0)))
    y = b
    for j in range(CONV_WIDTH):
        y = y + w[j] * up[:, j:j + S]
    return y

def second_inputs(seed: int = 0) -> dict:
    key = jax.random.key(seed)
    ks = jax.random.split(key, 24)

    def nrm(k, shape, scale):
        return jax.random.normal(k, shape, jnp.float32) * scale

    def gain(k, n):
        return 1.0 + nrm(k, (DEPTH, n), 0.05)

    return {
        "x": nrm(ks[0], (BATCH, SEQ, D_MODEL), 1.0),
        "mem": nrm(ks[1], (BATCH, MEM_TOKENS, D_MODEL), 1.0),
        "norm_mix_pre": gain(ks[2], D_MODEL),
        "w_in": nrm(ks[3], (DEPTH, D_MODEL, IN_COLS_2), D_MODEL ** -0.5),
        "lambda_q1": nrm(ks[4], (DEPTH, DH_DIFF), 0.1),
        "lambda_k1": nrm(ks[5], (DEPTH, DH_DIFF), 0.1),
        "lambda_q2": nrm(ks[6], (DEPTH, DH_DIFF), 0.1),
        "lambda_k2": nrm(ks[7], (DEPTH, DH_DIFF), 0.1),
        "subln_g": gain(ks[8], 2 * DH_DIFF),
        "w_attn_branch": nrm(ks[9], (DEPTH, DIFF_V_WIDTH, D_MODEL), DIFF_V_WIDTH ** -0.5),
        "pool_w": nrm(ks[10], (DEPTH, POOL_GROUPS, POOL_GROUP_WIDTH, POOL_GROUP_WIDTH), POOL_GROUP_WIDTH ** -0.5),
        "pool_scale": gain(ks[11], POOL_WIDTH),
        "w_pool_branch": nrm(ks[12], (DEPTH, POOL_WIDTH, D_MODEL), POOL_WIDTH ** -0.5),
        "norm_mem": gain(ks[13], D_MODEL),
        "w_mem_kv": nrm(ks[14], (DEPTH, D_MODEL, 2 * MEM_WIDTH), D_MODEL ** -0.5),
        "w_mem_branch": nrm(ks[15], (DEPTH, MEM_WIDTH, D_MODEL), MEM_WIDTH ** -0.5),
        "w_out": nrm(ks[16], (DEPTH, D_MODEL, D_MODEL), D_MODEL ** -0.5),
        "norm_mix_post": gain(ks[17], D_MODEL),
        "norm_ffn_pre": gain(ks[18], D_MODEL),
        "w_up": nrm(ks[19], (DEPTH, D_MODEL, 2 * D_FF_2), D_MODEL ** -0.5),
        "conv_w": nrm(ks[20], (DEPTH, CONV_WIDTH, 2 * D_FF_2), CONV_WIDTH ** -0.5),
        "conv_b": nrm(ks[21], (DEPTH, 2 * D_FF_2), 0.02),
        "w_down": nrm(ks[22], (DEPTH, D_FF_2, D_MODEL), D_FF_2 ** -0.5),
        "norm_ffn_post": gain(ks[23], D_MODEL),
    }

def second_block(x, mem, norm_mix_pre, w_in, lambda_q1, lambda_k1, lambda_q2, lambda_k2, subln_g,
              w_attn_branch, pool_w, pool_scale, w_pool_branch, norm_mem, w_mem_kv, w_mem_branch,
              w_out, norm_mix_post, norm_ffn_pre, w_up, conv_w, conv_b, w_down, norm_ffn_post):
    B, S, D = x.shape
    split_pts = np.cumsum([DIFF_Q_WIDTH, DIFF_Q_WIDTH, DIFF_V_WIDTH, POOL_WIDTH, MEM_WIDTH]).tolist()
    for l in range(DEPTH):
        lam_init = lambda_init_for(l)
        h = rms_norm(x, norm_mix_pre[l])
        proj = h @ w_in[l]
        q_d, k_d, v_d, u_p, q_m, gate_logits = jnp.split(proj, split_pts, axis=-1)

        lam = (jnp.exp(jnp.sum(lambda_q1[l].astype(jnp.float32) * lambda_k1[l].astype(jnp.float32)))
               - jnp.exp(jnp.sum(lambda_q2[l].astype(jnp.float32) * lambda_k2[l].astype(jnp.float32)))
               + lam_init)
        q_d = q_d.reshape(B, S, N_DIFF_HEADS, 2, DH_DIFF)
        k_d = k_d.reshape(B, S, N_DIFF_HEADS, 2, DH_DIFF)
        v_d = v_d.reshape(B, S, N_DIFF_HEADS, 2 * DH_DIFF)
        a = diff_attention(q_d, k_d, v_d, lam)
        a = rms_norm(a, subln_g[l]) * (1.0 - lam_init)
        y_attn = a.reshape(B, S, DIFF_V_WIDTH).astype(x.dtype) @ w_attn_branch[l]

        y_pool = multiscale_pool(u_p, pool_w[l], pool_scale[l]) @ w_pool_branch[l]

        mem_n = rms_norm(mem, norm_mem[l])
        y_mem = memory_cross_attention_2(q_m, mem_n, w_mem_kv[l]) @ w_mem_branch[l]

        gates = jax.nn.sigmoid(gate_logits.astype(jnp.float32)).reshape(B, S, N_BRANCHES, D).astype(x.dtype)
        mix = gates[:, :, 0] * y_attn + gates[:, :, 1] * y_pool + gates[:, :, 2] * y_mem
        x = x + rms_norm(mix @ w_out[l], norm_mix_post[l])

        h2 = rms_norm(x, norm_ffn_pre[l])
        up = causal_depthwise_conv(h2 @ w_up[l], conv_w[l], conv_b[l])
        g, v = jnp.split(up, 2, axis=-1)
        ff = (jax.nn.gelu(g, approximate=True) * v) @ w_down[l]
        x = x + rms_norm(ff, norm_ffn_post[l])
    return x


def setup_inputs(seed=0):
    out = dict(first_inputs(seed))
    for name, value in second_inputs(seed + 1).items():
        if name != "x":
            out[name + "_2"] = value
    return out


def reference(
    x, mem, norm_mix_g, w_in, fox_f_bias, hgrn_lb_logits, hgrn_norm_g, w_out, norm_x_g,
    norm_mem_g, w_xq, w_xkv, w_xo, norm_ff_g, w1, w2, final_norm_g, mem_2, norm_mix_pre_2,
    w_in_2, lambda_q1_2, lambda_k1_2, lambda_q2_2, lambda_k2_2, subln_g_2, w_attn_branch_2,
    pool_w_2, pool_scale_2, w_pool_branch_2, norm_mem_2, w_mem_kv_2, w_mem_branch_2, w_out_2,
    norm_mix_post_2, norm_ffn_pre_2, w_up_2, conv_w_2, conv_b_2, w_down_2, norm_ffn_post_2,
):
    x = first_block(
        x, mem, norm_mix_g, w_in, fox_f_bias, hgrn_lb_logits, hgrn_norm_g, w_out, norm_x_g,
        norm_mem_g, w_xq, w_xkv, w_xo, norm_ff_g, w1, w2, final_norm_g,
    )
    return second_block(
        x, mem_2, norm_mix_pre_2, w_in_2, lambda_q1_2, lambda_k1_2, lambda_q2_2, lambda_k2_2,
        subln_g_2, w_attn_branch_2, pool_w_2, pool_scale_2, w_pool_branch_2, norm_mem_2,
        w_mem_kv_2, w_mem_branch_2, w_out_2, norm_mix_post_2, norm_ffn_pre_2, w_up_2, conv_w_2,
        conv_b_2, w_down_2, norm_ffn_post_2,
    )


_drawn_inputs = setup_inputs


def setup_inputs(seed=0):
    import zlib

    import numpy as np

    out = dict(_drawn_inputs(seed))
    spreads = {}
    factors = {'norm_mix_g': 2.892,
     'hgrn_lb_logits': 8.0,
     'hgrn_norm_g': 5.323,
     'norm_x_g': 8.0,
     'norm_mem_g': 8.0,
     'lambda_q1_2': 64.0,
     'lambda_k1_2': 3.225,
     'lambda_q2_2': 22.04,
     'norm_mem_2': 8.0,
     'conv_b_2': 3.411,
     'norm_ff_g': 8.0,
     'lambda_k2_2': 8.0,
     'subln_g_2': 8.0,
     'pool_scale_2': 8.0}
    for name, (base, spread) in spreads.items():
        noise = np.random.default_rng([zlib.crc32(name.encode()), seed]).standard_normal(out[name].shape)
        drawn = base * np.exp(spread * noise) if base else spread * noise
        out[name] = __import__('jax').numpy.asarray(drawn.astype(out[name].dtype))
    for name, factor in factors.items():
        out[name] = (out[name] * factor).astype(out[name].dtype)
    return out
```

```python
from contextlib import ExitStack

import concourse.bass as bass
from concourse import mybir

F32 = mybir.dt.float32
F32R = mybir.dt.float32r
U32 = mybir.dt.uint32
BF16 = mybir.dt.bfloat16
ALU = mybir.AluOpType
ACT = mybir.ActivationFunctionType
AX = mybir.AxisListType.X

P = 128
D = 1024
KT = D // P
T = 256
TT = T // P
FOX = 512
FOX_H = 8
HG_H = 4
FF1 = 4096
FF2 = 2816
NT2 = FF2 // P
RING = 3
SLAB = 2048
NEG = -1e30
EPS = 1e-6
LN_MIN = 2.0 ** -64
LAM_INIT = 0.2
ALIBI = [2.0 ** -(h + 1) for h in range(8)]
POOL_W = (2, 4, 8, 16)
PAD = 16


def plan(w):
    slabs, first = [], {}

    def cols(name, wt, c0, n, nk=8, c=256, evac="act", k0=0):
        first[name] = len(slabs)
        for j in range(n):
            ap = wt[k0 * P:(k0 + nk) * P, c0 + j * c:c0 + (j + 1) * c].rearrange("(k p) c -> p k c", p=P)
            slabs.append(("T", ap, nk, c, evac))

    def half(name, wt, c0, n, evac="act"):
        first[name] = len(slabs)
        for j in range(n):
            for k in range(2):
                ap = wt[k * 512:(k + 1) * 512, c0 + j * 512:c0 + (j + 1) * 512].rearrange("(k p) c -> p k c", p=P)
                slabs.append(("N", ap, 4, 512, evac if k else None))

    def rows(name, wt, n, evac="dve"):
        first[name] = len(slabs)
        for j in range(n):
            ap = wt[j * 256:(j + 1) * 256, :].rearrange("(k p) c -> p k c", p=P)
            slabs.append(("N", ap, 2, 1024, evac if j == n - 1 else None))

    wi = w["w_in"]
    cols("gf", wi, 2056, 2, evac="act")
    cols("gq", wi, 1544, 2, evac="dve")
    cols("ff", wi, 1536, 1, c=128, evac="dve")
    cols("fq", wi, 0, 2)
    cols("fk", wi, 512, 2)
    half("fv", wi, 1024, 1)
    half("gi", wi, 2568, 1)
    half("gg", wi, 3080, 1, evac="dve")
    cols("xk", w["w_xkv"], 0, 4)
    half("xv", w["w_xkv"], D, 2)
    cols("km", w["w_mem_kv_2"], 0, 2)
    half("vm", w["w_mem_kv_2"], 512, 1)
    rows("wo", w["w_out"], 4)
    cols("xq", w["w_xq"], 0, 4)
    rows("xo", w["w_xo"], 4)
    cols("w1", w["w1"], 0, 16)
    rows("w2", w["w2"], 16)
    wi = w["w_in_2"]
    cols("qd", wi, 0, 4)
    cols("kd", wi, 1024, 4)
    rows("vd", wi[:, 2048:3072], 4, evac="act")
    cols("up", wi, 3072, 2)
    cols("qm", wi, 3584, 2)
    cols("ga", wi, 4096, 12)
    cols("pb", w["w_pool_branch_2"], 0, 2, nk=4, c=512, evac="dve")
    cols("mb", w["w_mem_branch_2"], 0, 2, nk=4, c=512, evac="dve")
    cols("ab", w["w_attn_branch_2"], 0, 4, evac="dve")
    rows("w3", w["w_out_2"], 4)
    first["cv"] = len(slabs)
    for j in range(NT2):
        ap = w["w_up_2"].rearrange("(k p) (two c) -> p k two c", p=P, two=2)[:, :, :, j * P:(j + 1) * P]
        slabs.append(("T", ap, 8, 256, "dve"))
    rows("wd", w["w_down_2"], NT2 // 2)
    return slabs, first


def two_blocks(nc, w, out):
    w = dict(w)
    for k in ("x", "mem", "mem_2", "w_in", "w_out", "w_xq", "w_xkv", "w_xo", "w1", "w2", "w_in_2", "w_attn_branch_2",
              "w_pool_branch_2", "w_mem_kv_2", "w_mem_branch_2", "w_out_2", "w_up_2", "w_down_2"):
        w[k] = w[k][0]
    slabs, first = plan(w)
    NS = len(slabs)
    act_evacs, dve_evacs, a, d = [], [], 0, 0
    for s in slabs:
        a, d = a + (s[4] == "act"), d + (s[4] == "dve")
        act_evacs.append(a)
        dve_evacs.append(d)

    landed = [0] * NS
    for n in range(NS):
        landed[n] = (landed[n - RING] if n >= RING else 0) + (16 if n < first["cv"] else 32)

    with ExitStack() as ctx:
        def sem(name):
            return ctx.enter_context(nc.semaphore(name))

        def sb(name, shape, dt=F32, at=None):
            return (at or ctx).enter_context(nc.sbuf_tensor(name, shape, dt))

        def sems(prefix, names):
            return {n: sem(f"{prefix}_{n}") for n in names.split()}

        raw = sb("raw", [P, RING, SLAB])
        whi = sb("whi", [P, RING, SLAB], F32R)
        wlo = sb("wlo", [P, RING, SLAB], F32R)
        xhi = sb("xhi", [P, KT, T], F32R)
        xlo = sb("xlo", [P, KT, T], F32R)
        h = sb("h", [P, TT, D])
        xn = sb("xn", [P, TT, D])
        junk = sb("junk", [P, D], BF16)
        kmT = sb("kmT", [P, 4, T])
        vm = sb("vm", [P, TT, 512])
        ident = sb("ident", [P, P])
        cols = sb("cols", [P, 256])
        negF = sb("negF", [P, T])
        ss = sb("ss", [P, 10, 2])
        rs = sb("rs", [P, 10, 2])
        half_neg = sb("half_neg", [P, 16])
        small = sb("small", [P, 64])
        mx = sb("mx", [P, 4, 4])
        nmx = sb("nmx", [P, 4, 4])
        den = sb("den", [P, 4, 4])
        rden = sb("rden", [P, 4, 4])

        with ExitStack() as st:
            xkT = sb("xkT", [P, KT, T], at=st)
            xv = sb("xv", [P, TT, D], at=st)
            with ExitStack() as r1:
                fqT = sb("fqT", [P, 4, T], at=r1)
                fkT = sb("fkT", [P, 4, T], at=r1)
                fv = sb("fv", [P, TT, FOX], at=r1)
                gi = sb("gi", [P, TT, FOX], at=r1)
                gg = sb("gg", [P, TT, FOX], at=r1)
                qs = sb("qs", [P, HG_H * T], at=r1)
                kk = sb("kk", [P, HG_H * T], at=r1)
                bb = sb("bb", [P, HG_H * T], at=r1)
                dz = sb("dz", [P, 2, HG_H * T], at=r1)
                am = sb("am", [P, 12, P], at=r1)
                fs = sb("fs", [P, 2, 384], at=r1)
                fpt = sb("fpt", [P, 2, 384], at=r1)
                mhi = sb("mhi", [P, KT, T], F32R, at=r1)
                mlo = sb("mlo", [P, KT, T], F32R, at=r1)
                lvl = sb("lvl", [P, 7, P], at=r1)
                causal = sb("causal", [P, 384], at=r1)
            with ExitStack() as r2:
                xqT = sb("xqT", [P, KT, T], at=r2)
                cs = sb("cs", [P, 4, 512], at=r2)
                cpt = sb("cpt", [P, 2, 512], at=r2)
        with ExitStack() as r3:
            hid_hi = sb("hid_hi", [P, FF1 // P, T], F32R, at=r3)
            hid_lo = sb("hid_lo", [P, FF1 // P, T], F32R, at=r3)
            ru = sb("ru", [P, 512], at=r3)
            sq = sb("sq", [P, 512], at=r3)
            gbc = sb("gbc", [P, D], at=r3)
        with ExitStack() as r4:
            qdT = sb("qdT", [P, KT, T], at=r4)
            kdT = sb("kdT", [P, KT, T], at=r4)
            vd = sb("vd", [P, TT, D], at=r4)
            upad = sb("upad", [P, 4, PAD + T], at=r4)
            uw = sb("uw", [P, 2, PAD + T], at=r4)
            qmT = sb("qmT", [P, 4, T], at=r4)
            gates = sb("gates", [P, 24, T], at=r4)
            phi = sb("phi", [P, 4, T], F32R, at=r4)
            plo = sb("plo", [P, 4, T], F32R, at=r4)
            ohi = sb("ohi", [P, 4, T], F32R, at=r4)
            olo = sb("olo", [P, 4, T], F32R, at=r4)
            ndist = sb("ndist", [P, 384], at=r4)
            ds_ = sb("ds_", [P, 2, 384], at=r4)
            dpt = sb("dpt", [P, 384], at=r4)
            ms = sb("ms", [P, 512], at=r4)
            mpt = sb("mpt", [P, 512], at=r4)
            pw = sb("pw", [P, 4, P], at=r4)
            rcnt = sb("rcnt", [P, PAD], at=r4)
        with ExitStack() as r5:
            gpost = sb("gpost", [P, D], at=r5)
            yhi = sb("yhi", [P, KT, T], F32R, at=r5)
            ylo = sb("ylo", [P, KT, T], F32R, at=r5)
            mixf = sb("mixf", [P, 512], at=r5)
            vhi = sb("vhi", [P, NT2, T], F32R, at=r5)
            vlo = sb("vlo", [P, NT2, T], F32R, at=r5)
            cy = sb("cy", [P, RING, 2, T], at=r5)
            cg = sb("cg", [P, T], at=r5)
            cf = sb("cf", [P, T], at=r5)

        tb = ctx.enter_context(nc.psum_tensor("tb", [P, 4, 512], F32))
        acc = ctx.enter_context(nc.psum_tensor("acc", [P, 2, TT, 512], F32))

        names = ["norm_mix_g", "norm_x_g", "norm_mem_g", "norm_ff_g", "norm_mix_pre_2", "norm_mem_2", "norm_ffn_pre_2"]
        C = {n: 8 * i for i, n in enumerate(names)}
        C["pool_scale_2"], C["lb"], C["hgrn_norm_g"], C["subln_g_2"], C["conv_b_2"] = 56, 60, 68, 69, 70
        C["conv_w_2"] = 114
        NC0, NCW = 114, 132

        raw_landed = [sem(f"raw_landed{i}") for i in range(RING)]
        hi_ready, lo_ready, slab_done = sem("hi_ready"), sem("lo_ready"), sem("slab_done")
        act_emptied, dve_emptied = sem("act_emptied"), sem("dve_emptied")
        x_in, rows_in, lam_in, bias_in, mem_in, mem2_in = (sem(n) for n in "x_in rows_in lam_in bias_in mem_in mem2_in".split())
        pw_in, gfin_in, gpost_in, gpost2_in, stored = (sem(n) for n in "pw_in gfin_in gpost_in gpost2_in stored".split())
        act_link, dve_link, pool_link = sem("act_link"), sem("dve_link"), sem("pool_link")
        consts_ready, cols_t, cols_ready, lam_ready, lb_ready = (
            sem(n) for n in "consts_ready cols_t cols_ready lam_ready lb_ready".split())
        nrm = sems("nrm", "src ss rs xn")
        fil = sems("fil", "t hi lo")
        hg = sems("hg", "sig f ln b sq qs d e z prod merged out sq2 ss rs rec rd gsig gg kk")
        fx = sems("fx", "z ea l F")
        fox = sems("fox", "scores read max exp p pt ptc pv pvhi pvlo")
        cr = sems("cr", "scores max exp p pt ptc pv pvhi pvlo")
        df = sems("df", "scores read max exp p pt ptc pv o")
        me = sems("me", "scores max exp p pt ptc pv pvhi pvlo")
        ffn = sems("ffn", "relu sq hi lo")
        pl = sems("pl", "ready mm hi lo")
        lamx, oss, ors, gx, gates_ready = (sem(n) for n in "lamx oss ors gx gates_ready".split())
        mix = sems("mix", "f hi lo")
        cvs = sems("cvs", "base tap1 y gelu f hi lo")

        FILL, g0 = {}, 0
        for name, n in (("x", 4), ("mem", 4), ("mem2", 4), ("rec", 2), ("h1", 4), ("h2", 4), ("x2", 4), ("a", 4), ("h4", 4)):
            FILL[name] = (g0, n)
            g0 += n
        NORM = {n: i for i, n in enumerate(["x", "mem", "mem2", "h1", "h2", "h3", "x2", "mix", "h4", "end"])}
        SRC = {n: 2 * i for i, n in enumerate(["h1", "h2", "h3", "x2", "h4", "end"])}
        ROWS = {n: 2 * (i + 1) for i, n in enumerate(["x", "mem", "mem2", "h1", "h2", "x2", "h4"])}
        LEVELS = 9

        def slab(t, n, nk):
            return t[:, n % RING, :nk * slabs[n][3]].rearrange("p (k c) -> p k c", k=nk)

        def fill_bank(name, g):
            return acc[:, 0, g % 2, :] if name == "a" else tb[:, 2 + g % 2, :]

        def halves(t, tt):
            return t[:, tt, :].rearrange("p (c n) -> p c n", c=2)

        def lvl_view(t, m):
            half = 1 << (m - 1)
            return t.rearrange("p (g r u) -> p g r u", r=2, u=half)

        block = ctx.enter_context(nc.Block())

        @block.sync
        def _(sp):
            def load(n, src=None, wait=None):
                if n >= RING:
                    sp.wait_ge(lo_ready, n - RING + 1 if wait is None else wait)
                _, ap, nk, c, _ = slabs[n]
                dst, src = slab(raw, n, nk), ap if src is None else src
                if n < first["cv"]:
                    sp.dma_start(dst, src).then_inc(raw_landed[n % RING], 16)
                    return
                for part in range(2):
                    if len(src.shape) == 4:
                        d, s = dst[:, :, part * P:part * P + P], src[:, :, part, :]
                    else:
                        d, s = dst[:, part, :], src[:, part, :]
                    sp.dma_start(d, s).then_inc(raw_landed[n % RING], 16)

            def loop(name, src, iters):
                n0 = first[name]
                with sp.Fori(0, iters) as i:
                    for u in range(RING):
                        load(n0 + u, src(i, u), i * RING + (n0 + u - RING + 1))

            for n in range(first["w1"]):
                load(n)
            w1v = w["w1"].rearrange("(k p) c -> p k c", p=P)
            loop("w1", lambda i, u: w1v[:, :, bass.ds(i * 768 + u * 256, 256)], 5)
            load(first["w1"] + 15)
            w2v = w["w2"].rearrange("(j k p) c -> p j k c", p=P, k=2)
            loop("w2", lambda i, u: w2v[:, bass.ds(i * 3 + u, 1), :, :].rearrange("p j k c -> p (j k) c"), 5)
            load(first["w2"] + 15)
            for n in range(first["qd"], first["cv"]):
                load(n)
            upv = w["w_up_2"].rearrange("(k p) (two c) -> p k two c", p=P, two=2)
            loop("cv", lambda i, u: upv[:, :, :, bass.ds(i * 384 + u * 128, 128)], 7)
            for n in range(first["cv"] + 21, NS):
                load(n)

        @block.gpsimd
        def _(pool):
            count = [0]

            def link(ins):
                count[0] += 1
                ins.then_inc(pool_link, 1)
                pool.wait_ge(pool_link, count[0])

            def select(t, pattern, base, chan, op, fill):
                link(pool.affine_select(out=t, in_=t, compare_op=op, fill=fill, base=base, pattern=pattern,
                                        channel_multiplier=chan))

            pool.memset(half_neg[:, :], -0.5)
            pool.memset(negF[:, :], 0.0)
            pool.memset(lvl[:, :, :], 0.0)
            pool.memset(causal[:, :], 0.0)
            link(pool.memset(ident[:, :], 0.0))
            select(ident[:, :], [[-1, P]], 0, 1, ALU.not_equal, 1.0)
            select(causal[:, 0:P], [[-1, P]], 0, 1, ALU.is_ge, NEG)
            select(causal[:, 256:384], [[-1, P]], 0, 1, ALU.is_ge, NEG)
            pool.sem_inc(consts_ready, 1)

            def rms(name, n, count_by=D):
                k = NORM[name]
                pool.wait_ge(nrm["ss"], 2 * (k + 1))
                link(pool.tensor_scalar(rs[:, k, :], ss[:, k, :], 1.0 / count_by, EPS, ALU.mult, ALU.add))
                pool.tensor_tensor(rs[:, k, :], rs[:, k, :], half_neg[:, 0:2], ALU.pow).then_inc(nrm["rs"], 1)

            rms("x", 0)
            for m in range(1, 8):
                half = 1 << (m - 1)
                n = P // (2 * half)
                t = lvl[:, m - 1, :].rearrange("p (g r u) -> p g r u", r=2, u=half)[:, :, 1, :]
                link(pool.memset(t, 1.0))
                select(t, [[-2 * half, n], [0, half]], 0, 1, ALU.is_ge, 0.0)
                select(t, [[2 * half, n], [0, half]], half - 1, -1, ALU.is_ge, 0.0)
            pool.sem_inc(consts_ready, 1)
            pool.wait_ge(fil["t"], FILL["x"][0] + 4)
            pool.dma_start(xn[:, :, :], w["mem"].rearrange("(t p) c -> p t c", p=P)).then_inc(mem_in, 16)
            rms("mem", 1)
            pool.wait_ge(fil["t"], FILL["mem"][0] + 4)
            pool.dma_start(xn[:, :, :], w["mem_2"].rearrange("(t p) c -> p t c", p=P)).then_inc(mem2_in, 16)
            rms("mem2", 2)

            pool.wait_ge(hg["kk"], 2)
            pool.wait_ge(hg["qs"], 2)
            for m in range(1, LEVELS):
                pool.wait_ge(hg["e"], m)
                z = lvl_view(dz[:, m % 2, :], m)
                pool.tensor_tensor(z[:, :, 0, :], z[:, :, 0, :], lvl_view(kk[:, :], m)[:, :, 0, :], ALU.mult)
                pool.tensor_tensor(z[:, :, 1, :], z[:, :, 1, :], lvl_view(qs[:, :], m)[:, :, 1, :], ALU.mult)\
                    .then_inc(hg["z"], 1)
            pool.wait_ge(hg["ss"], 1)
            link(pool.tensor_scalar(small[:, 8:16], small[:, 0:8], 1.0 / P, EPS, ALU.mult, ALU.add))
            pool.tensor_tensor(small[:, 8:16], small[:, 8:16], half_neg[:, 0:8], ALU.pow).then_inc(hg["rs"], 1)
            rms("h1", 3)
            rms("h2", 4)
            pool.dma_start(gbc[:, :], w["final_norm_g"].rearrange("(a c) -> a c", a=1).broadcast_to([P, D])
                           ).then_inc(gfin_in, 16)
            rms("h3", 5)
            rms("x2", 6)
            pool.dma_start(pw[:, :, :], w["pool_w_2"][0].rearrange("g c d -> c g d")).then_inc(pw_in, 16)
            pool.memset(upad[:, :, 0:PAD], 0.0)
            pool.memset(uw[:, :, 0:PAD], 0.0)
            for c0, base in ((0, 0), (P, P), (2 * P, 0)):
                pool.iota(ndist[:, c0:c0 + P], [[1, P]], base=-base, channel_multiplier=-1,
                          allow_small_or_imprecise_dtypes=True)
            link(pool.iota(rcnt[:, :], [[1, PAD]], base=1, channel_multiplier=0, allow_small_or_imprecise_dtypes=True))
            select(ndist[:, 0:P], [[-1, P]], 0, 1, ALU.is_ge, NEG)
            select(ndist[:, 256:384], [[-1, P]], 0, 1, ALU.is_ge, NEG)
            link(pool.tensor_tensor(rcnt[:, :], rcnt[:, :], half_neg[:, :], ALU.pow))
            link(pool.tensor_tensor(rcnt[:, :], rcnt[:, :], rcnt[:, :], ALU.mult))
            pool.sem_inc(consts_ready, 1)
            pool.wait_ge(act_emptied, act_evacs[first["up"] + 1])
            for g, win in enumerate(POOL_W):
                src, width, b = upad[:, g, :], 1, 0
                while width < win:
                    dst = uw[:, b, :]
                    link(pool.tensor_tensor(dst[:, PAD:], src[:, PAD:], src[:, PAD - width:PAD + T - width], ALU.add))
                    src, width, b = dst, 2 * width, 1 - b
                n = win - 1
                dst = uw[:, b, :]
                pool.tensor_scalar(dst[:, PAD + n:], src[:, PAD + n:], 1.0 / win, 0.0, ALU.mult, ALU.add)
                link(pool.tensor_tensor(dst[:, PAD:PAD + n], src[:, PAD:PAD + n], rcnt[:, 0:n], ALU.mult))
                link(pool.tensor_tensor(upad[:, g, PAD:], dst[:, PAD:], upad[:, g, PAD:], ALU.subtract))
            pool.sem_inc(pl["ready"], 1)
            pool.wait_ge(oss, 1)
            link(pool.tensor_scalar(small[:, 32:48], small[:, 16:32], 1.0 / P, EPS, ALU.mult, ALU.add))
            pool.tensor_tensor(small[:, 32:48], small[:, 32:48], half_neg[:, :], ALU.pow).then_inc(ors, 1)
            pool.wait_ge(df["scores"], 8)
            pool.dma_start(gpost[:, :], w["norm_mix_post_2"].broadcast_to([P, D])).then_inc(gpost_in, 16)
            rms("mix", 7)
            rms("h4", 8)
            pool.dma_start(gpost[:, :], w["norm_ffn_post_2"].broadcast_to([P, D])).then_inc(gpost2_in, 16)
            rms("end", 9)

        @block.tensor
        def _(pe):
            def mm3(o, a_hi, a_lo, b_hi, b_lo, start, stop):
                pe.matmul(o, a_hi, b_hi, start=start, stop=False)
                pe.matmul(o, a_hi, b_lo, start=False, stop=False)
                return pe.matmul(o, a_lo, b_hi, start=False, stop=stop)

            def split_ready(n, value=None):
                pe.wait_ge(hi_ready, n + 1 if value is None else value)
                pe.wait_ge(lo_ready, n + 1 if value is None else value)

            def emptied(n):
                if slabs[n][4] == "act":
                    pe.wait_ge(act_emptied, act_evacs[n])
                else:
                    pe.wait_ge(dve_emptied, dve_evacs[n])

            def t_slab(n, hi, lo, bank, value=None):
                split_ready(n, value)
                nk = slabs[n][2]
                a_hi, a_lo = slab(whi, n, nk), slab(wlo, n, nk)
                for c in range(slabs[n][3] // P):
                    o = tb[:, bank + c // 2, (c % 2) * T:(c % 2) * T + T]
                    for k in range(nk):
                        last = mm3(o, a_hi[:, k, c * P:(c + 1) * P], a_lo[:, k, c * P:(c + 1) * P],
                                   hi[:, k, :], lo[:, k, :], k == 0, k == nk - 1)
                last.then_inc(slab_done, 1)

            def half_slab(n, hi, lo, k0, pair):
                split_ready(n)
                b_hi, b_lo = slab(whi, n, 4), slab(wlo, n, 4)
                for t in range(TT):
                    o = acc[:, pair, t, :]
                    for k in range(4):
                        a = (k0 + k, slice(t * P, t * P + P))
                        last = mm3(o, hi[:, a[0], a[1]], lo[:, a[0], a[1]], b_hi[:, k, :], b_lo[:, k, :],
                                   k0 + k == 0, k0 + k == 7)
                last.then_inc(slab_done, 1)

            def row_slab(n, hi, lo, k0, nk_all):
                split_ready(n)
                b_hi, b_lo = slab(whi, n, 2), slab(wlo, n, 2)
                for t in range(TT):
                    for c in range(2):
                        o = acc[:, c, t, :]
                        for k in range(2):
                            a = slice(t * P, t * P + P)
                            last = mm3(o, hi[:, k0 + k, a], lo[:, k0 + k, a], b_hi[:, k, c * 512:c * 512 + 512],
                                       b_lo[:, k, c * 512:c * 512 + 512], k0 + k == 0, k0 + k == nk_all - 1)
                last.then_inc(slab_done, 1)

            def fill(name, src):
                g0, n = FILL[name]
                for g in range(g0, g0 + n):
                    if g >= 2:
                        pe.wait_ge(fil["lo"], g - 1)
                    o = fill_bank(name, g)
                    for k in range(2):
                        for t in range(TT):
                            last = pe.transpose(o[:, k * T + t * P:k * T + t * P + P],
                                                src[:, t, ((g - g0) * 2 + k) * P:((g - g0) * 2 + k + 1) * P], ident[:, :])
                    last.then_inc(fil["t"], 1)

            def filled(name):
                g0, n = FILL[name]
                pe.wait_ge(fil["hi"], g0 + n)
                pe.wait_ge(fil["lo"], g0 + n)

            pe.wait_ge(consts_ready, 1)
            pe.wait_ge(rows_in, 16 * 12)
            pe.wait_ge(bias_in, 48)
            pe.transpose(acc[:, 0, 0, 0:NC0], fs[0:NC0, 0, 0:P], ident[0:NC0, 0:NC0])
            for i in range(2):
                last = pe.transpose(acc[:, 0, 0, NC0 + 66 * i:NC0 + 66 * i + 66], fs[0:66, 0, P * (i + 1):P * (i + 2)],
                                    ident[0:66, 0:66])
            last.then_inc(cols_t, 1)
            pe.wait_ge(nrm["xn"], ROWS["x"])
            fill("x", xn)
            filled("x")

            A = first["gf"]
            for n in range(A, first["fv"]):
                if n >= 2:
                    emptied(n - 2)
                t_slab(n, xhi, xlo, n % 2)
                if n == 2:
                    pe.wait_ge(nrm["xn"], ROWS["mem"])
                    fill("mem", xn)
            pe.wait_ge(cols_ready, 1)
            for j, name in enumerate(("fv", "gi", "gg")):
                if name == "gg":
                    emptied(first["fv"] + 1)
                for k in range(2):
                    half_slab(first[name] + k, xhi, xlo, 4 * k, j % 2)

            def fox_scores(i):
                if i == 0:
                    emptied(first["fk"] + 1)
                    pe.wait_ge(fx["F"], 1)
                    pe.wait_ge(fil["lo"], FILL["mem"][0] + 4)
                pe.wait_ge(fox["read"], i) if i else None
                p0, c = (i % 2) * 64, i // 2
                for o, s, t in ((tb[:, 2, 0:P], P, 0), (tb[:, 2, P:384], T, 1)):
                    pe.matmul(o, ident[:, i:i + 1].broadcast_to([P, P]), negF[:, 0:s], start=True, stop=False)
                    last = pe.matmul(o, fqT[p0:p0 + 64, c, t * P:t * P + P], fkT[p0:p0 + 64, c, 0:s], start=False, stop=True)
                last.then_inc(fox["scores"], 1)

            def fox_transpose(i):
                pe.wait_ge(fox["p"], i + 1)
                if i:
                    pe.wait_ge(fox["pvlo"], i)
                for b in range(3):
                    last = pe.transpose(tb[:, 3, b * P:b * P + P], fs[:, i % 2, b * P:b * P + P], ident[:, :])
                last.then_inc(fox["pt"], 1)

            def fox_values(i):
                pe.wait_ge(fox["ptc"], i + 1)
                if i == 0:
                    emptied(first["fv"] + 1)
                p0 = (i % 2) * 64
                o, pt = tb[p0:p0 + 64, 3, :], fpt[:, i % 2, :]
                v = slice(i * 64, i * 64 + 64)
                pe.matmul(o[:, 0:P], fv[:, 0, v], pt[:, 0:P], start=True, stop=True)
                pe.matmul(o[:, P:T], fv[:, 0, v], pt[:, P:T], start=True, stop=False)
                pe.matmul(o[:, P:T], fv[:, 1, v], pt[:, T:384], start=False, stop=True).then_inc(fox["pv"], 1)

            def hg_products(m):
                if m == 0:
                    pe.wait_ge(hg["kk"], 2)
                    pe.wait_ge(hg["qs"], 2)
                    emptied(first["gi"] + 1)
                else:
                    pe.wait_ge(hg["z"], m)
                    pe.wait_ge(hg["merged"], m)
                z = dz[:, m % 2, :]
                a, b = (kk, qs) if m == 0 else (z, z)
                for i in range(HG_H):
                    if m == LEVELS - 1:
                        last = pe.matmul(acc[:, 1, 0, i * P:i * P + P], z[:, i * T:i * T + P],
                                         z[:, i * T + P:i * T + T], start=True, stop=True)
                        continue
                    for t in range(TT):
                        s = slice(i * T + t * P, i * T + t * P + P)
                        last = pe.matmul(acc[:, 1, t, i * P:i * P + P], a[:, s], b[:, s], start=True, stop=True)
                last.then_inc(hg["prod"], 1)

            def hg_out():
                pe.wait_ge(hg["merged"], LEVELS)
                for i in range(HG_H):
                    v = slice(i * P, i * P + P)
                    pe.matmul(acc[:, 1, 0, v], am[:, i, :], gi[:, 0, v], start=True, stop=True)
                    pe.matmul(acc[:, 1, 1, v], am[:, 8 + i, :], gi[:, 0, v], start=True, stop=False)
                    last = pe.matmul(acc[:, 1, 1, v], am[:, 4 + i, :], gi[:, 1, v], start=False, stop=True)
                last.then_inc(hg["out"], 1)

            filled("mem")
            B = first["xk"]
            for i in range(12):
                n = B + i
                if i == 8:
                    fox_transpose(7)
                    fox_values(7)
                    pe.wait_ge(nrm["xn"], ROWS["mem2"])
                    pe.wait_ge(fox["pvlo"], 8)
                    fill("mem2", xn)
                    hg_products(8)
                    filled("mem2")
                if n < first["xv"]:
                    emptied(n - 2 if i >= 2 else first["fk"] + i)
                    t_slab(n, mhi, mlo, n % 2)
                elif n < first["km"]:
                    if i == 4:
                        emptied(first["gg"] + 1)
                    elif i == 6:
                        emptied(first["xv"] + 1)
                    half_slab(n, mhi, mlo, 4 * (i % 2), 0)
                elif n < first["vm"]:
                    emptied(first["xk"] + 2 + n - first["km"])
                    t_slab(n, mhi, mlo, n % 2)
                else:
                    if i == 10:
                        emptied(first["xv"] + 3)
                    half_slab(n, mhi, mlo, 4 * (i % 2), 0)
                if i < 8:
                    if i:
                        fox_transpose(i - 1)
                    fox_scores(i)
                    hg_products(i)
                    if i:
                        fox_values(i - 1)
                elif i == 9:
                    hg_out()
                elif i == 11:
                    pe.wait_ge(hg["rec"], 1)
                    fill("rec", dz[:, 1, :].rearrange("p (t c) -> p t c", t=TT))

            emptied(first["vm"] + 1)
            pe.wait_ge(hg["rd"], 1)
            pe.wait_ge(fox["pvlo"], 8)
            for j in range(4):
                if j == 2:
                    filled("rec")
                row_slab(first["wo"] + j, xhi, xlo, 2 * j, 8)
            pe.wait_ge(nrm["xn"], ROWS["h1"])
            fill("h1", xn)
            filled("h1")

            def cross_scores(i):
                emptied(first["xq"] + i)
                for t in range(TT):
                    o = acc[:, i // 2, i % 2, t * T:t * T + T]
                    for k in range(2):
                        last = pe.matmul(o, xqT[:, 2 * i + k, t * P:t * P + P], xkT[:, 2 * i + k, :], start=k == 0, stop=k == 1)
                last.then_inc(cr["scores"], 1)

            def cross_transpose(i):
                pe.wait_ge(cr["p"], i + 1)
                if i >= 2:
                    pe.wait_ge(cr["ptc"], i - 1)
                for mt in range(TT):
                    for t in range(TT):
                        last = pe.transpose(tb[:, 2 + i % 2, mt * T + t * P:mt * T + t * P + P],
                                            cs[:, i, t * T + mt * P:t * T + mt * P + P], ident[:, :])
                last.then_inc(cr["pt"], 1)

            def cross_values(i):
                pe.wait_ge(cr["ptc"], i + 1)
                if i >= 2:
                    pe.wait_ge(cr["pvlo"], i - 1)
                for dt in range(2):
                    for mt in range(TT):
                        last = pe.matmul(tb[:, i % 2, dt * T:dt * T + T], xv[:, mt, i * T + dt * P:i * T + dt * P + P],
                                         cpt[:, i % 2, mt * T:mt * T + T], start=mt == 0, stop=mt == 1)
                last.then_inc(cr["pv"], 1)

            pe.wait_ge(dve_emptied, dve_evacs[first["wo"] + 3])
            for j in range(4):
                n = first["xq"] + j
                emptied(n - 2 if j >= 2 else first["km"] + j)
                t_slab(n, xhi, xlo, n % 2)
                if j:
                    cross_scores(j - 1)
            cross_scores(3)
            for j in range(4):
                cross_transpose(j)
                if j:
                    cross_values(j - 1)
            cross_values(3)
            for j in range(4):
                pe.wait_ge(cr["pvlo"], j + 1)
                row_slab(first["xo"] + j, xhi, xlo, 2 * j, 8)
            pe.wait_ge(nrm["xn"], ROWS["h2"])
            fill("h2", xn)
            filled("h2")

            def t_loop(name, iters):
                n0 = first[name]
                done = (act_emptied, act_evacs) if slabs[n0][4] == "act" else (dve_emptied, dve_evacs)
                with pe.Fori(0, iters) as i:
                    for u in range(RING):
                        pe.wait_ge(done[0], i * RING + (done[1][n0 + u] - RING))
                        t_slab(n0 + u, xhi, xlo, u, i * RING + (n0 + u + 1))

            t_loop("w1", 5)
            n = first["w1"] + 15
            pe.wait_ge(act_emptied, act_evacs[n - RING])
            t_slab(n, xhi, xlo, 0)
            for j in range(16):
                pe.wait_ge(ffn["lo"], j + 1)
                row_slab(first["w2"] + j, hid_hi, hid_lo, 2 * j, 32)
            pe.wait_ge(nrm["xn"], ROWS["x2"])
            fill("x2", xn)
            filled("x2")

            for n in range(first["qd"], first["vd"]):
                if n >= first["qd"] + 2:
                    emptied(n - 2)
                t_slab(n, xhi, xlo, n % 2)
            for j in range(4):
                row_slab(first["vd"] + j, xhi, xlo, 2 * j, 8)

            def diff_scores(i):
                if i == 0:
                    emptied(first["kd"] + 3)
                if i:
                    pe.wait_ge(df["read"], 2 * i)
                for c in range(2):
                    p0 = 64 * c
                    pe.matmul(tb[:, 2 + c, 0:P], qdT[p0:p0 + 64, i, 0:P], kdT[p0:p0 + 64, i, 0:P], start=True, stop=True)
                    last = pe.matmul(tb[:, 2 + c, P:384], qdT[p0:p0 + 64, i, P:T], kdT[p0:p0 + 64, i, 0:T],
                                     start=True, stop=True)
                last.then_inc(df["scores"], 1)

            def diff_transpose(i):
                pe.wait_ge(df["p"], i + 1)
                if i:
                    pe.wait_ge(df["ptc"], i)
                else:
                    emptied(first["vd"] + 3)
                for b in range(3):
                    last = pe.transpose(acc[:, 0, 0, b * P:b * P + P], ds_[:, 0, b * P:b * P + P], ident[:, :])
                last.then_inc(df["pt"], 1)

            def diff_values(i):
                pe.wait_ge(df["ptc"], i + 1)
                if i:
                    pe.wait_ge(df["o"], i)
                v = slice(i * P, i * P + P)
                pe.matmul(acc[:, 0, 1, 0:P], dpt[:, 0:P], vd[:, 0, v], start=True, stop=True)
                pe.matmul(acc[:, 0, 1, P:T], dpt[:, P:T], vd[:, 0, v], start=True, stop=False)
                pe.matmul(acc[:, 0, 1, P:T], dpt[:, T:384], vd[:, 1, v], start=False, stop=True).then_inc(df["pv"], 1)

            def mem_scores(i):
                if i:
                    pe.wait_ge(me["exp"], i)
                else:
                    emptied(first["qm"] + 1)
                for t in range(TT):
                    last = pe.matmul(acc[:, 1, 0, t * T:t * T + T], qmT[:, i, t * P:t * P + P], kmT[:, i, :], start=True, stop=True)
                last.then_inc(me["scores"], 1)

            def mem_transpose(i):
                pe.wait_ge(me["p"], i + 1)
                if i:
                    pe.wait_ge(me["ptc"], i)
                for mt in range(TT):
                    for t in range(TT):
                        last = pe.transpose(acc[:, 1, 1, mt * T + t * P:mt * T + t * P + P],
                                            ms[:, t * T + mt * P:t * T + mt * P + P], ident[:, :])
                last.then_inc(me["pt"], 1)

            def mem_values(i):
                pe.wait_ge(me["ptc"], i + 1)
                if i:
                    pe.wait_ge(me["pvlo"], i)
                for mt in range(TT):
                    last = pe.matmul(acc[:, 0, 1, 0:T], vm[:, mt, i * P:i * P + P], mpt[:, mt * T:mt * T + T],
                                     start=mt == 0, stop=mt == 1)
                last.then_inc(me["pv"], 1)

            for i in range(16):
                n = first["up"] + i
                emptied(n - 2 if i >= 2 else first["kd"] + 2 + i)
                t_slab(n, xhi, xlo, n % 2)
                if 1 <= i <= 8:
                    diff_transpose(i - 1)
                if i < 8:
                    diff_scores(i)
                if 1 <= i <= 8:
                    diff_values(i - 1)
                if i == 9:
                    pe.wait_ge(df["o"], 8)
                if 9 <= i <= 12:
                    mem_transpose(i - 9)
                if 10 <= i <= 13:
                    mem_values(i - 10)
                if 8 <= i <= 11:
                    mem_scores(i - 8)
                if i == 14:
                    pe.wait_ge(me["pvlo"], 4)
                    pe.wait_ge(pw_in, 16)
                    pe.wait_ge(pl["ready"], 1)
                    for g in range(4):
                        last = pe.matmul(acc[:, 0, g // 2, (g % 2) * T:(g % 2) * T + T], pw[:, g, :], upad[:, g, PAD:], start=True, stop=True)
                    last.then_inc(pl["mm"], 1)
            pe.wait_ge(pl["lo"], 1)
            pe.wait_ge(df["read"], 16)
            for j in range(2):
                if j == 0:
                    emptied(first["ga"] + 10)
                    emptied(first["ga"] + 11)
                t_slab(first["pb"] + j, phi, plo, 2 * j)
            pe.wait_ge(gx, 1)
            fill("a", xn)
            pe.wait_ge(me["pvlo"], 4)
            for j in range(2):
                emptied(first["pb"] + j)
                t_slab(first["mb"] + j, ohi, olo, 2 * j)
            filled("a")
            emptied(first["mb"])
            for j in range(4):
                if j >= 2:
                    emptied(first["ab"] + j - 2)
                t_slab(first["ab"] + j, xhi, xlo, j % 2)
            for j in range(4):
                pe.wait_ge(mix["lo"], j + 1)
                row_slab(first["w3"] + j, yhi, ylo, 2 * j, 8)
            pe.wait_ge(nrm["xn"], ROWS["h4"])
            fill("h4", xn)
            filled("h4")
            t_loop("cv", 7)
            n = first["cv"] + 21
            pe.wait_ge(dve_emptied, dve_evacs[n - RING])
            t_slab(n, xhi, xlo, 0)
            pe.wait_ge(dve_emptied, dve_evacs[first["w3"] + 3])
            for j in range(NT2 // 2):
                pe.wait_ge(cvs["lo"], 2 * j + 2)
                row_slab(first["wd"] + j, vhi, vlo, 2 * j, NT2)

        @block.scalar
        def _(act):
            count = [0]

            def link(ins):
                count[0] += 1
                ins.then_inc(act_link, 1)
                act.wait_ge(act_link, count[0])

            def hi(n, value=None):
                if n >= NS:
                    return
                if value is None:
                    act.wait_ge(raw_landed[n % RING], landed[n])
                    if n >= RING:
                        act.wait_ge(slab_done, n - RING + 1)
                else:
                    act.wait_ge(raw_landed[n % RING], value[0])
                    act.wait_ge(slab_done, value[1])
                m = slabs[n][2] * slabs[n][3]
                act.activation(whi[:, n % RING, :m], raw[:, n % RING, :m], ACT.Copy).then_inc(hi_ready, 1)

            def loop_hi(i, n):
                hi(n, (i * (landed[n] - landed[n - RING]) + landed[n], i * RING + (n - RING + 1)))

            def empty(n, out, func=ACT.Copy, src=None, **kw):
                act.wait_ge(slab_done, n + 1)
                return act.activation(out, src, func, **kw)

            def tbank(n):
                return tb[:, n % 2, :]

            def sumsq(name, src=None):
                k = NORM[name]
                for t in range(TT):
                    if src is None:
                        act.wait_ge(nrm["src"], SRC[name] + t + 1)
                    if k or t:
                        act.wait_ge(nrm["ss"], 2 * k + t)
                    act.activation(junk[:, :], (h if src is None else src)[:, t, :] if src is not acc else acc[:, :, t, :], ACT.Square,
                                   accum_out=ss[:, k, t:t + 1]).then_inc(nrm["ss"], 1)

            def fill(name, dst, gain, k0=0, shared=False):
                g0, n = FILL[name]
                for g in range(g0, g0 + n):
                    act.wait_ge(fil["t"], g + 1)
                    o = fill_bank(name, g)
                    for k in range(2):
                        kt = k0 + (g - g0) * 2 + k
                        c = gain if shared else gain + kt
                        last = act.activation(dst[:, kt, :], o[:, k * T:k * T + T], ACT.Copy, scale=cols[:, c:c + 1])
                    last.then_inc(fil["hi"], 1)

            act.dma_start(h[:, :, :], w["x"].rearrange("(t p) c -> p t c", p=P)).then_inc(x_in, 16)
            for n in names:
                act.dma_start(fs[C[n]:C[n] + 8, 0, 0:P], w[n].rearrange("a (k p) -> (a k) p", p=P)).then_inc(rows_in, 16)
            act.dma_start(fs[56:60, 0, 0:P], w["pool_scale_2"].rearrange("a (k p) -> (a k) p", p=P)).then_inc(rows_in, 16)
            act.dma_start(fs[60:68, 0, 0:P], w["hgrn_lb_logits"].rearrange("a (k p) -> (a k) p", p=P)).then_inc(rows_in, 16)
            act.dma_start(fs[68:69, 0, 0:P], w["hgrn_norm_g"]).then_inc(rows_in, 16)
            act.dma_start(fs[69:70, 0, 0:P], w["subln_g_2"]).then_inc(rows_in, 16)
            act.dma_start(fs[70:114, 0, 0:P], w["conv_b_2"].rearrange("a (k p) -> (a k) p", p=P)).then_inc(rows_in, 16)
            cw = w["conv_w_2"].rearrange("a j (k p) -> (a j k) p", p=P)
            act.dma_start(fs[0:66, 0, P:T], cw[0:66, :]).then_inc(bias_in, 16)
            act.dma_start(fs[0:66, 0, T:384], cw[66:132, :]).then_inc(bias_in, 16)
            act.dma_start(small[0:8, 59:60], w["fox_f_bias"].rearrange("a h -> h a"),
                          allow_slow_non_contiguous=True).then_inc(bias_in, 16)
            for i, n in enumerate(("lambda_q1_2", "lambda_k1_2", "lambda_q2_2", "lambda_k2_2")):
                act.dma_start(fpt[:, 0, 64 * i:64 * i + 64], w[n].broadcast_to([P, 64])).then_inc(lam_in, 16)

            act.wait_ge(x_in, 16)
            sumsq("x", h)
            for n in range(RING):
                hi(n)
            act.wait_ge(cols_ready, 1)
            fill("x", xhi, C["norm_mix_g"])
            act.wait_ge(lb_ready, 1)
            act.activation(small[:, 52:56], small[:, 48:52], ACT.Sigmoid).then_inc(lb_ready, 1)

            A = first["gf"]
            for j in range(2):
                empty(A + j, dz[:, 0, j * 512:j * 512 + 512], ACT.Sigmoid, tbank(A + j)).then_inc(act_emptied, 1)
                hi(A + j + RING)
            for j in range(2):
                n = first["gq"] + j
                empty(n, dz[:, 1, j * 512:j * 512 + 512], ACT.Sigmoid, tbank(n)).then_inc(hg["sq"], 1)
                hi(n + RING)
                if j == 0:
                    act.wait_ge(mem_in, 16)
                    sumsq("mem", xn)
                    fill("mem", mhi, C["norm_mem_g"])
            act.wait_ge(hg["kk"], 2)
            act.activation(bb[:, :], dz[:, 0, :], ACT.Ln).then_inc(hg["ln"], 1)
            act.wait_ge(fx["z"], 1)
            link(act.activation(am[0:8, 2, :], am[0:8, 0, :], ACT.Exp, scale=-1.0))
            link(act.activation(am[0:8, 3, :], am[0:8, 1, :], ACT.Exp, scale=-1.0))
            act.activation(am[0:8, 2:4, :], am[0:8, 2:4, :], ACT.Ln, bias=1.0).then_inc(fx["l"], 1)
            hi(first["ff"] + RING)
            act.wait_ge(mem2_in, 16)
            sumsq("mem2", xn)
            act.wait_ge(lamx, 1)
            act.activation(rden[:, 3, 0:2], den[:, 3, 0:2], ACT.Exp).then_inc(lam_ready, 1)
            for j in range(2):
                n = first["fq"] + j
                empty(n, fqT[:, 2 * j:2 * j + 2, :], ACT.Copy, tbank(n), scale=0.125).then_inc(act_emptied, 1)
                hi(n + RING)
            for j in range(2):
                n = first["fk"] + j
                empty(n, fkT[:, 2 * j:2 * j + 2, :], ACT.Copy, tbank(n)).then_inc(act_emptied, 1)
                hi(n + RING)
            for j, (name, dst) in enumerate((("fv", fv), ("gi", gi))):
                n = first[name] + 1
                hi(n - 1 + RING)
                empty(n, dst[:, :, :], ACT.Copy, acc[:, j, :, :]).then_inc(act_emptied, 1)
                hi(n + RING)
            n = first["gg"] + 1
            hi(n - 1 + RING)
            empty(n, gg[:, :, :], ACT.Sigmoid, acc[:, 0, :, :]).then_inc(hg["gsig"], 1)
            hi(n + RING)

            def fox_exp(i):
                act.wait_ge(fox["max"], i + 1)
                s = fs[:, i % 2, :]
                act.activation(s[:, 0:P], s[:, 0:P], ACT.Exp, bias=nmx[:, i % 2, 0:1], accum_out=den[:, i % 2, 0:1])
                act.activation(s[:, P:384], s[:, P:384], ACT.Exp, bias=nmx[:, i % 2, 1:2], accum_out=den[:, i % 2, 1:2])\
                    .then_inc(fox["exp"], 1)

            def fox_copy(i):
                act.wait_ge(fox["pt"], i + 1)
                if i >= 2:
                    act.wait_ge(fox["pv"], i - 1)
                act.activation(fpt[:, i % 2, :], tb[:, 3, 0:384], ACT.Copy).then_inc(fox["ptc"], 1)

            def fox_hi(i):
                p0 = (i % 2) * 64
                act.wait_ge(fox["pv"], i + 1)
                act.activation(xhi[p0:p0 + 64, i // 2, :], tb[p0:p0 + 64, 3, 0:T], ACT.Copy).then_inc(fox["pvhi"], 1)

            def hg_exp(m):
                act.wait_ge(hg["d"], m)
                z = lvl_view(dz[:, m % 2, :], m)
                act.activation(z[:, :, 0, :], z[:, :, 0, :], ACT.Exp, scale=-1.0)
                src = lvl_view(bb[:, :], m) if m == LEVELS - 1 else z
                act.activation(z[:, :, 1, :], src[:, :, 1, :], ACT.Exp).then_inc(hg["e"], 1)

            B = first["xk"]
            hg_exp(1)
            for i in range(12):
                n = B + i
                if i == 8:
                    fox_copy(7)
                    fox_hi(7)
                    fill("mem2", mhi, C["norm_mem_2"])
                if n < first["xv"]:
                    empty(n, xkT[:, 2 * i:2 * i + 2, :], ACT.Copy, tbank(n)).then_inc(act_emptied, 1)
                elif n < first["km"]:
                    if i % 2:
                        c = (i - 5) // 2 * 512
                        empty(n, xv[:, :, c:c + 512], ACT.Copy, acc[:, 0, :, :]).then_inc(act_emptied, 1)
                elif n < first["vm"]:
                    j = n - first["km"]
                    empty(n, kmT[:, 2 * j:2 * j + 2, :], ACT.Copy, tbank(n)).then_inc(act_emptied, 1)
                elif i == 11:
                    empty(n, vm[:, :, :], ACT.Copy, acc[:, 0, :, :]).then_inc(act_emptied, 1)
                hi(n + RING)
                if i < 8:
                    if i:
                        fox_copy(i - 1)
                    fox_exp(i)
                    if 2 <= i + 1 <= 8:
                        hg_exp(i + 1)
                    if i:
                        fox_hi(i - 1)
                elif i == 9:
                    act.wait_ge(hg["out"], 1)
                    act.activation(dz[:, 1, :], acc[:, 1, :, :], ACT.Square).then_inc(hg["sq2"], 1)
                elif i == 11:
                    fill("rec", xhi, C["hgrn_norm_g"], k0=4, shared=True)

            for j in range(4):
                hi_n = first["wo"] + j + RING
                if j < 3:
                    hi(hi_n)
            sumsq("h1")
            hi(first["wo"] + 3 + RING)
            fill("h1", xhi, C["norm_x_g"])

            def cross_exp(i):
                act.wait_ge(cr["max"], i + 1)
                for t in range(TT):
                    o = acc[:, i // 2, i % 2, t * T:t * T + T]
                    last = act.activation(cs[:, i, t * T:t * T + T], o, ACT.Exp, bias=nmx[:, i, t:t + 1], scale=1.0 / 16,
                                          accum_out=den[:, i, t:t + 1])
                last.then_inc(cr["exp"], 1)

            def cross_copy(i):
                act.wait_ge(cr["pt"], i + 1)
                if i >= 2:
                    act.wait_ge(cr["pv"], i - 1)
                act.activation(cpt[:, i % 2, :], tb[:, 2 + i % 2, :], ACT.Copy).then_inc(cr["ptc"], 1)

            def cross_hi(i):
                act.wait_ge(cr["pv"], i + 1)
                act.activation(xhi[:, 2 * i:2 * i + 2, :], tb[:, i % 2, :], ACT.Copy).then_inc(cr["pvhi"], 1)

            for j in range(4):
                n = first["xq"] + j
                empty(n, xqT[:, 2 * j:2 * j + 2, :], ACT.Copy, tbank(n)).then_inc(act_emptied, 1)
                hi(n + RING)
                if j >= 2:
                    cross_exp(j - 2)
            cross_exp(2)
            cross_copy(0)
            cross_exp(3)
            for j in range(1, 4):
                cross_copy(j)
                cross_hi(j - 1)
            cross_hi(3)
            for j in range(4):
                if j < 3:
                    hi(first["xo"] + j + RING)
            sumsq("h2")
            hi(first["xo"] + 3 + RING)
            fill("h2", xhi, C["norm_ff_g"])

            def relu_step(bank, done, j, dst):
                act.wait_ge(slab_done, done)
                act.activation(ru[:, :], tb[:, bank, :], ACT.Relu).then_inc(act_emptied, 1)

            def relu_hi(dst, sq_count):
                act.wait_ge(ffn["sq"], sq_count)
                act.activation(dst, sq[:, :], ACT.Copy).then_inc(ffn["hi"], 1)

            n0 = first["w1"]
            with act.Fori(0, 5) as i:
                for u in range(RING):
                    relu_step(u, i * RING + (n0 + u + 1), None, None)
                    loop_hi(i, n0 + u + RING)
                    relu_hi(hid_hi[:, bass.ds(i * 6 + 2 * u, 2), :], i * RING + (u + 1))
            relu_step(0, n0 + 16, None, None)
            hi(n0 + 15 + RING)
            relu_hi(hid_hi[:, 30:32, :], 16)
            n0 = first["w2"]
            with act.Fori(0, 4) as i:
                for u in range(RING):
                    loop_hi(i, n0 + u + RING)
            for j in range(12, 15):
                hi(n0 + j + RING)
            sumsq("h3")
            hi(n0 + 15 + RING)
            sumsq("x2")
            fill("x2", xhi, C["norm_mix_pre_2"])

            for j in range(4):
                n = first["qd"] + j
                empty(n, qdT[:, 2 * j:2 * j + 2, :], ACT.Copy, tbank(n), scale=0.125).then_inc(act_emptied, 1)
                hi(n + RING)
            for j in range(4):
                n = first["kd"] + j
                empty(n, kdT[:, 2 * j:2 * j + 2, :], ACT.Copy, tbank(n)).then_inc(act_emptied, 1)
                hi(n + RING)
            for j in range(4):
                n = first["vd"] + j
                if j == 3:
                    act.wait_ge(slab_done, n + 1)
                    act.activation(vd[:, 0, :], acc[:, :, 0, :], ACT.Copy)
                    act.activation(vd[:, 1, :], acc[:, :, 1, :], ACT.Copy).then_inc(act_emptied, 1)
                hi(n + RING)

            def diff_exp(i):
                for c in range(2):
                    act.wait_ge(df["max"], 2 * i + c + 1)
                    s = ds_[:, c, :]
                    act.activation(s[:, 0:P], s[:, 0:P], ACT.Exp, bias=nmx[:, c, 0:1], accum_out=den[:, c, 0:1])
                    act.activation(s[:, P:384], s[:, P:384], ACT.Exp, bias=nmx[:, c, 1:2], accum_out=den[:, c, 1:2])\
                        .then_inc(df["exp"], 1)

            def diff_copy(i):
                act.wait_ge(df["pt"], i + 1)
                if i:
                    act.wait_ge(df["pv"], i)
                act.activation(dpt[:, :], acc[:, 0, 0, 0:384], ACT.Copy).then_inc(df["ptc"], 1)

            def diff_out(i):
                act.wait_ge(df["pv"], i + 1)
                act.activation(xn[:, :, i * P:i * P + P], acc[:, 0, 1, 0:T].rearrange("p (t c) -> p t c", t=2),
                               ACT.Copy).then_inc(df["o"], 1)

            def mem_exp(i):
                act.wait_ge(me["max"], i + 1)
                for t in range(TT):
                    last = act.activation(ms[:, t * T:t * T + T], acc[:, 1, 0, t * T:t * T + T], ACT.Exp,
                                          bias=nmx[:, 2, t:t + 1], scale=P ** -0.5, accum_out=den[:, 2, t:t + 1])
                last.then_inc(me["exp"], 1)

            def mem_copy(i):
                act.wait_ge(me["pt"], i + 1)
                if i:
                    act.wait_ge(me["pv"], i)
                act.activation(mpt[:, :], acc[:, 1, 1, :], ACT.Copy).then_inc(me["ptc"], 1)

            def mem_hi(i):
                act.wait_ge(me["pv"], i + 1)
                act.activation(ohi[:, i, :], acc[:, 0, 1, 0:T], ACT.Copy).then_inc(me["pvhi"], 1)

            for i in range(16):
                n = first["up"] + i
                if i < 2:
                    dst = upad[:, 2 * i:2 * i + 2, PAD:]
                    empty(n, dst, ACT.Copy, tbank(n).rearrange("p (k t) -> p k t", k=2)).then_inc(act_emptied, 1)
                elif i < 4:
                    empty(n, qmT[:, 2 * i - 4:2 * i - 2, :], ACT.Copy, tbank(n)).then_inc(act_emptied, 1)
                else:
                    empty(n, gates[:, 2 * i - 8:2 * i - 6, :], ACT.Copy if i < 12 else ACT.Sigmoid,
                          tbank(n)).then_inc(act_emptied, 1)
                if 1 <= i <= 8:
                    diff_copy(i - 1)
                if 9 <= i <= 12:
                    mem_copy(i - 9)
                hi(n + RING)
                if i < 8:
                    diff_exp(i)
                if 1 <= i <= 8:
                    diff_out(i - 1)
                if 10 <= i <= 13:
                    mem_hi(i - 10)
                if 8 <= i <= 11:
                    mem_exp(i - 8)
                if i >= 12:
                    s = gates[:, 4 * (i - 12):4 * (i - 11), :]
                    act.wait_ge(act_emptied, act_evacs[first["ga"] + 7])
                    act.activation(s, s, ACT.Sigmoid).then_inc(gates_ready, 1)
                if i == 14:
                    act.wait_ge(pl["mm"], 1)
                    for g in range(4):
                        c = C["pool_scale_2"] + g
                        last = act.activation(phi[:, g, :], acc[:, 0, g // 2, (g % 2) * T:(g % 2) * T + T], ACT.Copy, scale=cols[:, c:c + 1])
                    last.then_inc(pl["hi"], 1)
            hi(first["pb"] + RING)
            fill("a", xhi, C["subln_g_2"], shared=True)
            hi(first["pb"] + 1 + RING)
            for j in range(2):
                hi(first["mb"] + j + RING)

            def mix_hi(j):
                act.wait_ge(mix["f"], j + 1)
                act.activation(yhi[:, 2 * j:2 * j + 2, :], mixf[:, :], ACT.Copy).then_inc(mix["hi"], 1)

            for j in range(4):
                hi(first["ab"] + j + RING)
                mix_hi(j)
            for j in range(3):
                hi(first["w3"] + j + RING)
            act.wait_ge(slab_done, first["w3"] + 4)
            sumsq("mix", acc)
            hi(first["w3"] + 3 + RING)
            sumsq("h4")
            fill("h4", xhi, C["norm_ffn_pre_2"])

            def conv_base(b, done, j):
                act.wait_ge(slab_done, done)
                for g in range(2):
                    a = C["conv_w_2"] + 2 * 44 + g * NT2
                    c = C["conv_b_2"] + g * NT2
                    last = act.activation(cy[:, b, g, :], tb[:, b, g * T:g * T + T], ACT.Identity,
                                          scale=cols[:, bass.ds(j + a, 1)], bias=cols[:, bass.ds(j + c, 1)])
                last.then_inc(cvs["base"], 1)

            def conv_gelu(b, k):
                act.wait_ge(cvs["y"], k)
                act.activation(cg[:, :], cy[:, b, 0, :], ACT.Gelu_apprx_tanh).then_inc(cvs["gelu"], 1)

            def conv_hi(j, k):
                act.wait_ge(cvs["f"], k)
                act.activation(vhi[:, bass.ds(j, 1), :], cf[:, :], ACT.Copy).then_inc(cvs["hi"], 1)

            n0 = first["cv"]
            act.activation(small[:, 0:1], half_neg[:, 0:1], ACT.Gelu_apprx_tanh)
            conv_base(0, n0 + 1, 0)
            hi(n0 + RING)
            with act.Fori(0, 7) as i:
                for u in range(RING):
                    conv_base((u + 1) % RING, i * RING + (n0 + u + 2), i * RING + (u + 1))
                    conv_gelu(u, i * RING + (u + 1))
                    loop_hi(i, n0 + u + 1 + RING)
                    conv_hi(i * RING + u, i * RING + (u + 1))
            conv_gelu(0, 22)
            conv_hi(21, 22)
            for j in range(NT2 // 2):
                hi(first["wd"] + j + RING)
            act.wait_ge(slab_done, NS)
            sumsq("end", acc)
            for t in range(TT):
                act.wait_ge(nrm["src"], SRC["end"] + t + 1)
                act.dma_start(out[0, t * P:t * P + P, :], h[:, t, :]).then_inc(stored, 16)
            act.wait_ge(stored, 32)

        @block.vector
        def _(dve):
            count = [0]

            def link(ins):
                count[0] += 1
                ins.then_inc(dve_link, 1)
                dve.wait_ge(dve_link, count[0])

            def lo(n, value=None):
                if n >= NS:
                    return
                dve.wait_ge(hi_ready, n + 1 if value is None else value)
                m = slabs[n][2] * slabs[n][3]
                dve.tensor_tensor(wlo[:, n % RING, :m], raw[:, n % RING, :m], whi[:, n % RING, :m].bitcast(F32),
                                  ALU.subtract).then_inc(lo_ready, 1)

            def loop_lo(i, n):
                lo(n, i * RING + (n + 1))

            def norm_rows(name, src=None):
                k = NORM[name]
                dve.wait_ge(nrm["rs"], k + 1)
                if FILL_BEFORE[name] is not None:
                    dve.wait_ge(fil["t"], FILL_BEFORE[name])
                for t in range(TT):
                    dve.tensor_scalar(xn[:, t, :], (h if src is None else src)[:, t, :], rs[:, k, t:t + 1], None,
                                      ALU.mult).then_inc(nrm["xn"], 1)

            FILL_BEFORE = {"x": None, "mem": None, "mem2": None, "h1": FILL["mem2"][0] + 4, "h2": FILL["h1"][0] + 4,
                           "x2": FILL["h2"][0] + 4, "h4": FILL["a"][0] + 4}

            def fill(name, dst_hi, dst, gain, k0=0, shared=False):
                g0, n = FILL[name]
                for g in range(g0, g0 + n):
                    dve.wait_ge(fil["hi"], g + 1)
                    o = fill_bank(name, g)
                    for k in range(2):
                        kt = k0 + (g - g0) * 2 + k
                        c = gain if shared else gain + kt
                        last = dve.scalar_tensor_tensor(dst[:, kt, :], o[:, k * T:k * T + T], cols[:, c:c + 1],
                                                        dst_hi[:, kt, :].bitcast(F32), ALU.mult, ALU.subtract)
                    last.then_inc(fil["lo"], 1)

            def tbank(n):
                return tb[:, n % 2, :]

            def residual(n, name):
                dve.wait_ge(slab_done, n + 1)
                k = NORM[name]
                for t in range(TT):
                    last = dve.tensor_tensor(halves(h, t), acc[:, :, t, :], halves(h, t), ALU.add)
                    last.then_inc(nrm["src"], 1)
                dve.wait_ge(nrm["src"], SRC[name] + 2)
                dve.sem_inc(dve_emptied, 1)

            dve.wait_ge(consts_ready, 1)
            dve.wait_ge(lam_in, 64)
            lam = fpt[:, 0, 0:256].rearrange("p (a b c) -> p a b c", a=2, b=2)
            link(dve.tensor_tensor(fpt[:, 1, 0:128].rearrange("p (a c) -> p a c", a=2), lam[:, :, 0, :], lam[:, :, 1, :],
                                   ALU.mult))
            dve.tensor_reduce(den[:, 3, 0:2], fpt[:, 1, 0:128].rearrange("p (a c) -> p a c", a=2), AX, ALU.add)\
                .then_inc(lamx, 1)
            dve.wait_ge(cols_t, 1)
            dve.tensor_copy(cols[:, 0:NC0 + NCW], acc[:, 0, 0, 0:NC0 + NCW]).then_inc(cols_ready, 1)
            norm_rows("x")
            dve.wait_ge(cols_ready, 1)
            dve.tensor_tensor(small[:, 48:52], cols[:, C["lb"]:C["lb"] + 4], cols[:, C["lb"] + 4:C["lb"] + 8],
                              ALU.subtract).then_inc(lb_ready, 1)
            for n in range(RING):
                lo(n)
            fill("x", xhi, xlo, C["norm_mix_g"])
            dve.wait_ge(lb_ready, 2)
            link(dve.tensor_scalar(small[:, 48:52], small[:, 52:56], -1.0, 1.0, ALU.mult, ALU.add))
            dve.tensor_scalar(cols[:, 69:70], cols[:, 69:70], 1.0 - LAM_INIT, None, ALU.mult)

            A = first["gf"]
            for j in range(2):
                dve.wait_ge(act_emptied, act_evacs[A + j])
                for i in range(2):
                    s = slice(j * 512 + i * T, j * 512 + i * T + T)
                    hd = 2 * j + i
                    last = dve.tensor_scalar(dz[:, 0, s], dz[:, 0, s], small[:, 48 + hd:49 + hd], small[:, 52 + hd:53 + hd],
                                             ALU.mult, ALU.add)
                link(last)
                s = slice(j * 512, j * 512 + 512)
                link(dve.tensor_scalar(kk[:, s], dz[:, 0, s], -1.0, 1.0, ALU.mult, ALU.add))
                dve.tensor_scalar(dz[:, 0, s], dz[:, 0, s], LN_MIN, None, ALU.max).then_inc(hg["kk"], 1)
                lo(A + j + RING)
            for j in range(2):
                n = first["gq"] + j
                dve.wait_ge(hg["sq"], j + 1)
                dve.tensor_tensor(qs[:, j * 512:j * 512 + 512], tbank(n), dz[:, 1, j * 512:j * 512 + 512], ALU.mult)\
                    .then_inc(hg["qs"], 1)
                dve.wait_ge(hg["qs"], j + 1)
                dve.sem_inc(dve_emptied, 1)
                lo(n + RING)
                if j == 0:
                    norm_rows("mem", xn)
                    fill("mem", mhi, mlo, C["norm_mem_g"])
            n = first["ff"]
            dve.wait_ge(slab_done, n + 1)
            dve.wait_ge(bias_in, 48)
            zf, az, mz = (am[0:8, i:i + 2, :].rearrange("p a c -> p (a c)") for i in (6, 0, 4))
            link(dve.tensor_scalar(zf, tb[0:8, n % 2, 0:T], small[0:8, 59:60], None, ALU.add))
            dve.sem_inc(dve_emptied, 1)
            dve.tensor_scalar(mz, zf, 0.0, None, ALU.min)
            dve.scalar_tensor_tensor(az, zf, -1.0, zf, ALU.mult, ALU.max).then_inc(fx["z"], 1)
            dve.memset(dz[:, 1, 0:P], 0.0)
            link(dve.memset(am[0:8, 8:10, :], 0.0))
            dve.wait_ge(hg["ln"], 1)
            for s in range(8):
                last = dve.tensor_tensor_scan(dz[:, 0, s * P:s * P + P], bb[:, s * P:s * P + P], dz[:, 1, 0:P], 0.0,
                                              ALU.add, ALU.add)
            link(last)
            link(dve.tensor_copy(bb[:, :], dz[:, 0, :]))
            lo(first["ff"] + RING)
            dve.wait_ge(fx["l"], 1)
            lf = am[0:8, 2:4, :].rearrange("p a c -> p (a c)")
            link(dve.tensor_tensor(zf, lf, mz, ALU.subtract))
            dve.tensor_tensor_scan(negF[0:8, :], zf, am[0:8, 8:10, :].rearrange("p a c -> p (a c)"), 0.0, ALU.add, ALU.add)\
                .then_inc(fx["F"], 1)
            norm_rows("mem2", xn)
            dve.wait_ge(lam_ready, 1)
            link(dve.tensor_tensor(small[:, 56:57], rden[:, 3, 1:2], rden[:, 3, 0:1], ALU.subtract))
            link(dve.tensor_scalar(small[:, 56:57], small[:, 56:57], -LAM_INIT, None, ALU.add))
            for n in range(first["fq"], first["gg"] + 1):
                lo(n + RING)

            def hg_diff(m):
                if m >= 2:
                    dve.wait_ge(hg["prod"], m - 1)
                z, b = lvl_view(dz[:, m % 2, :], m), lvl_view(bb[:, :], m)
                half = 1 << (m - 1)
                if m == LEVELS - 1:
                    mid = b[:, :, 0, half - 1:half].broadcast_to([P, b.shape[1], half])
                    dve.tensor_tensor(z[:, :, 0, :], b[:, :, 0, :], mid, ALU.subtract).then_inc(hg["d"], 1)
                    return
                b3 = b.rearrange("p g r u -> p g (r u)")
                mid = b3[:, :, half - 1:half].broadcast_to([P, b.shape[1], 2 * half])
                dve.tensor_tensor(z.rearrange("p g r u -> p g (r u)"), b3, mid, ALU.subtract).then_inc(hg["d"], 1)

            hg_diff(1)
            n = first["gg"] + 1
            dve.wait_ge(hg["gsig"], 1)
            dve.tensor_tensor(gg[:, :, :], acc[:, 0, :, :], gg[:, :, :], ALU.mult).then_inc(hg["gg"], 1)
            dve.wait_ge(hg["gg"], 1)
            dve.sem_inc(dve_emptied, 1)
            lo(n + RING)

            def row_max(src, i, scale):
                dve.tensor_reduce(mx[:, i, 0:1], src[:, 0:P], AX, ALU.max)
                link(dve.tensor_reduce(mx[:, i, 1:2], src[:, P:384], AX, ALU.max))
                return dve.tensor_scalar(nmx[:, i, 0:2], mx[:, i, 0:2], -scale, None, ALU.mult)

            def fox_mask(i):
                dve.wait_ge(fox["scores"], i + 1)
                if i == 0:
                    dve.wait_ge(consts_ready, 2)
                if i >= 2:
                    dve.wait_ge(fox["pt"], i - 1)
                s = fs[:, i % 2, :]
                dve.tensor_tensor(s, tb[:, 2, 0:384], causal[:, :], ALU.add).then_inc(fox["read"], 1)
                dve.wait_ge(fox["read"], i + 1)
                row_max(s, i % 2, 1.0).then_inc(fox["max"], 1)

            def fox_norm(i):
                dve.wait_ge(fox["exp"], i + 1)
                link(dve.reciprocal(rden[:, i % 2, 0:2], den[:, i % 2, 0:2]))
                s = fs[:, i % 2, :]
                dve.tensor_scalar(s[:, 0:P], s[:, 0:P], rden[:, i % 2, 0:1], None, ALU.mult)
                dve.tensor_scalar(s[:, P:384], s[:, P:384], rden[:, i % 2, 1:2], None, ALU.mult).then_inc(fox["p"], 1)

            def fox_lo(i):
                p0 = (i % 2) * 64
                dve.wait_ge(fox["pvhi"], i + 1)
                dve.tensor_tensor(xlo[p0:p0 + 64, i // 2, :], tb[p0:p0 + 64, 3, 0:T],
                                  xhi[p0:p0 + 64, i // 2, :].bitcast(F32), ALU.subtract).then_inc(fox["pvlo"], 1)

            def hg_merge(m):
                dve.wait_ge(hg["prod"], m + 1)
                if m:
                    dve.wait_ge(hg["merged"], m)
                if m == LEVELS - 1:
                    dve.tensor_copy(am[:, 8:12, :], acc[:, 1, 0, :].rearrange("p (h t) -> p h t", h=4))\
                        .then_inc(hg["merged"], 1)
                    return
                for t in range(TT):
                    o = acc[:, 1, t, :].rearrange("p (h t) -> p h t", h=4)
                    dst = am[:, 4 * t:4 * t + 4, :]
                    if m == 0:
                        eye = ident[:, :].rearrange("p (a t) -> p a t", a=1).broadcast_to([P, 4, P])
                        last = dve.tensor_tensor(dst, o, eye, ALU.mult)
                    else:
                        mask = lvl[:, m - 1, :].bitcast(U32).rearrange("p (a t) -> p a t", a=1).broadcast_to([P, 4, P])
                        last = dve.copy_predicated(dst, mask, o)
                last.then_inc(hg["merged"], 1)

            B = first["xk"]
            for i in range(12):
                if i == 8:
                    fox_lo(7)
                    fill("mem2", mhi, mlo, C["norm_mem_2"])
                    hg_merge(8)
                lo(B + i + RING)
                if i < 8:
                    fox_mask(i)
                    if 2 <= i + 1 <= 8:
                        hg_diff(i + 1)
                    fox_norm(i)
                    hg_merge(i)
                    if i:
                        fox_lo(i - 1)
                elif i == 9:
                    dve.wait_ge(hg["sq2"], 1)
                    dve.tensor_reduce(small[:, 0:8], dz[:, 1, :].rearrange("p (g v) -> p g v", v=P), AX, ALU.add)\
                        .then_inc(hg["ss"], 1)
                    dve.wait_ge(hg["rs"], 1)
                    for t in range(TT):
                        r = small[:, 8 + 4 * t:12 + 4 * t].rearrange("p (h a) -> p h a", a=1).broadcast_to([P, 4, P])
                        last = dve.tensor_tensor(dz[:, 1, t * 512:t * 512 + 512].rearrange("p (h v) -> p h v", h=4),
                                                 acc[:, 1, t, :].rearrange("p (h v) -> p h v", h=4), r, ALU.mult)
                    last.then_inc(hg["rd"], 1)
                    dve.wait_ge(hg["rd"], 1)
                    dve.tensor_tensor(dz[:, 1, :], dz[:, 1, :], gg[:, :, :].rearrange("p t c -> p (t c)"), ALU.mult)\
                        .then_inc(hg["rec"], 1)
                elif i == 11:
                    fill("rec", xhi, xlo, C["hgrn_norm_g"], k0=4, shared=True)

            for j in range(3):
                lo(first["wo"] + j + RING)
            residual(first["wo"] + 3, "h1")
            norm_rows("h1")
            lo(first["wo"] + 3 + RING)
            fill("h1", xhi, xlo, C["norm_x_g"])

            def cross_max(i):
                dve.wait_ge(cr["scores"], i + 1)
                src = acc[:, i // 2, i % 2, :].rearrange("p (t m) -> p t m", t=2)
                link(dve.tensor_reduce(mx[:, i, 0:2], src, AX, ALU.max))
                dve.tensor_scalar(nmx[:, i, 0:2], mx[:, i, 0:2], -1.0 / 16, None, ALU.mult).then_inc(cr["max"], 1)

            def cross_norm(i):
                dve.wait_ge(cr["exp"], i + 1)
                link(dve.reciprocal(rden[:, i, 0:2], den[:, i, 0:2]))
                for t in range(TT):
                    last = dve.tensor_scalar(cs[:, i, t * T:t * T + T], cs[:, i, t * T:t * T + T], rden[:, i, t:t + 1], None,
                                             ALU.mult)
                last.then_inc(cr["p"], 1)

            def cross_lo(i):
                dve.wait_ge(cr["pvhi"], i + 1)
                dve.tensor_tensor(xlo[:, 2 * i:2 * i + 2, :], tb[:, i % 2, :], xhi[:, 2 * i:2 * i + 2, :].bitcast(F32),
                                  ALU.subtract).then_inc(cr["pvlo"], 1)

            for j in range(4):
                lo(first["xq"] + j + RING)
                if j >= 2:
                    cross_max(j - 2)
                    cross_norm(j - 2)
            cross_max(2)
            cross_max(3)
            cross_norm(2)
            cross_norm(3)
            for j in range(4):
                cross_lo(j)
            for j in range(3):
                lo(first["xo"] + j + RING)
            residual(first["xo"] + 3, "h2")
            norm_rows("h2")
            lo(first["xo"] + 3 + RING)
            fill("h2", xhi, xlo, C["norm_ff_g"])

            def square(emptied):
                dve.wait_ge(act_emptied, emptied)
                dve.tensor_tensor(sq[:, :], ru[:, :], ru[:, :], ALU.mult).then_inc(ffn["sq"], 1)

            def square_lo(dst, src_hi, k):
                dve.wait_ge(ffn["hi"], k)
                dve.tensor_tensor(dst, sq[:, :], src_hi.bitcast(F32), ALU.subtract).then_inc(ffn["lo"], 1)
                dve.wait_ge(ffn["lo"], k)

            n0 = first["w1"]
            with dve.Fori(0, 5) as i:
                for u in range(RING):
                    square(i * RING + act_evacs[n0 + u])
                    loop_lo(i, n0 + u + RING)
                    s = bass.ds(i * 6 + 2 * u, 2)
                    square_lo(hid_lo[:, s, :], hid_hi[:, s, :], i * RING + (u + 1))
            square(act_evacs[n0 + 15])
            lo(n0 + 15 + RING)
            square_lo(hid_lo[:, 30:32, :], hid_hi[:, 30:32, :], 16)
            n0 = first["w2"]
            with dve.Fori(0, 4) as i:
                for u in range(RING):
                    loop_lo(i, n0 + u + RING)
            for j in range(12, 15):
                lo(n0 + j + RING)
            residual(n0 + 15, "h3")
            dve.wait_ge(nrm["rs"], NORM["h3"] + 1)
            dve.wait_ge(gfin_in, 16)
            for t in range(TT):
                dve.scalar_tensor_tensor(h[:, t, :], h[:, t, :], rs[:, NORM["h3"], t:t + 1], gbc[:, :], ALU.mult, ALU.mult)\
                    .then_inc(nrm["src"], 1)
            norm_rows("x2")
            lo(n0 + 15 + RING)
            fill("x2", xhi, xlo, C["norm_mix_pre_2"])

            for n in range(first["qd"], first["up"]):
                lo(n + RING)

            def diff_mask(i):
                for c in range(2):
                    if c == 0:
                        dve.wait_ge(df["scores"], i + 1)
                        if i:
                            dve.wait_ge(df["pt"], i)
                        else:
                            dve.wait_ge(consts_ready, 3)
                    s = ds_[:, c, :]
                    dve.scalar_tensor_tensor(s, ndist[:, :], ALIBI[i], tb[:, 2 + c, 0:384], ALU.mult, ALU.add)\
                        .then_inc(df["read"], 1)
                    dve.wait_ge(df["read"], 2 * i + c + 1)
                    row_max(s, c, 1.0).then_inc(df["max"], 1)

            def diff_combine(i):
                dve.wait_ge(df["exp"], 2 * i + 2)
                link(dve.reciprocal(rden[:, 0:2, 0:2], den[:, 0:2, 0:2]))
                s0, s1 = ds_[:, 0, :], ds_[:, 1, :]
                dve.tensor_scalar(s0[:, 0:P], s0[:, 0:P], rden[:, 0, 0:1], None, ALU.mult)
                dve.tensor_scalar(s0[:, P:384], s0[:, P:384], rden[:, 0, 1:2], None, ALU.mult)
                link(dve.tensor_scalar(rden[:, 1, 0:2], rden[:, 1, 0:2], small[:, 56:57], None, ALU.mult))
                dve.scalar_tensor_tensor(s0[:, 0:P], s1[:, 0:P], rden[:, 1, 0:1], s0[:, 0:P], ALU.mult, ALU.add)
                dve.scalar_tensor_tensor(s0[:, P:384], s1[:, P:384], rden[:, 1, 1:2], s0[:, P:384], ALU.mult, ALU.add)\
                    .then_inc(df["p"], 1)

            def mem_max(i):
                dve.wait_ge(me["scores"], i + 1)
                src = acc[:, 1, 0, :].rearrange("p (t m) -> p t m", t=2)
                link(dve.tensor_reduce(mx[:, 2, 0:2], src, AX, ALU.max))
                dve.tensor_scalar(nmx[:, 2, 0:2], mx[:, 2, 0:2], -(P ** -0.5), None, ALU.mult).then_inc(me["max"], 1)

            def mem_norm(i):
                dve.wait_ge(me["exp"], i + 1)
                link(dve.reciprocal(rden[:, 2, 0:2], den[:, 2, 0:2]))
                for t in range(TT):
                    last = dve.tensor_scalar(ms[:, t * T:t * T + T], ms[:, t * T:t * T + T], rden[:, 2, t:t + 1], None, ALU.mult)
                last.then_inc(me["p"], 1)

            def mem_lo(i):
                dve.wait_ge(me["pvhi"], i + 1)
                dve.tensor_tensor(olo[:, i, :], acc[:, 0, 1, 0:T], ohi[:, i, :].bitcast(F32), ALU.subtract)\
                    .then_inc(me["pvlo"], 1)

            o16 = xn[:, :, :].rearrange("p t (h e) -> p t h e", h=8)
            for i in range(16):
                if i < 8:
                    diff_mask(i)
                if 8 <= i <= 11:
                    mem_max(i - 8)
                lo(first["up"] + i + RING)
                if i < 8:
                    diff_combine(i)
                if 10 <= i <= 13:
                    mem_lo(i - 10)
                if 8 <= i <= 11:
                    mem_norm(i - 8)
                if i == 9:
                    dve.wait_ge(df["o"], 8)
                    sqv = qdT[:, :, :].rearrange("p k t -> p (k t)")
                    link(dve.tensor_tensor(sqv, xn[:, :, :].rearrange("p t c -> p (t c)"),
                                           xn[:, :, :].rearrange("p t c -> p (t c)"), ALU.mult))
                    dve.tensor_reduce(small[:, 16:32], sqv.rearrange("p (g e) -> p g e", e=P), AX, ALU.add).then_inc(oss, 1)
                if i == 10:
                    dve.wait_ge(ors, 1)
                    for t in range(TT):
                        r = small[:, 32 + 8 * t:40 + 8 * t].rearrange("p (h a) -> p h a", a=1).broadcast_to([P, 8, P])
                        last = dve.tensor_tensor(o16[:, t], o16[:, t], r, ALU.mult)
                    last.then_inc(gx, 1)
                if i == 14:
                    dve.wait_ge(pl["hi"], 1)
                    for g in range(4):
                        c = C["pool_scale_2"] + g
                        last = dve.scalar_tensor_tensor(plo[:, g, :], acc[:, 0, g // 2, (g % 2) * T:(g % 2) * T + T], cols[:, c:c + 1],
                                                        phi[:, g, :].bitcast(F32), ALU.mult, ALU.subtract)
                    last.then_inc(pl["lo"], 1)

            gt = gates[:, :, :].rearrange("p k t -> p (k t)")

            def times_gate(n, bank, g, width):
                dve.wait_ge(slab_done, n + 1)
                dve.wait_ge(gates_ready, 4)
                s = slice(g * T, g * T + width)
                src = tb[:, bank:bank + width // 512, :].rearrange("p b c -> p (b c)")
                link(dve.tensor_tensor(gt[:, s], src, gt[:, s], ALU.mult))
                dve.sem_inc(dve_emptied, 1)

            times_gate(first["pb"], 0, 8, 1024)
            lo(first["pb"] + RING)
            fill("a", xhi, xlo, C["subln_g_2"], shared=True)
            times_gate(first["pb"] + 1, 2, 12, 1024)
            lo(first["pb"] + 1 + RING)
            for j in range(2):
                times_gate(first["mb"] + j, 2 * j, 16 + 4 * j, 1024)
                lo(first["mb"] + j + RING)
                a, b = slice((8 + 4 * j) * T, (12 + 4 * j) * T), slice((16 + 4 * j) * T, (20 + 4 * j) * T)
                link(dve.tensor_tensor(gt[:, a], gt[:, a], gt[:, b], ALU.add))
            for j in range(4):
                times_gate(first["ab"] + j, j % 2, 2 * j, 512)
                a, b = slice(2 * j * T, (2 * j + 2) * T), slice((8 + 2 * j) * T, (10 + 2 * j) * T)
                dve.tensor_tensor(mixf[:, :], gt[:, a], gt[:, b], ALU.add).then_inc(mix["f"], 1)
                lo(first["ab"] + j + RING)
                dve.wait_ge(mix["hi"], j + 1)
                dve.tensor_tensor(ylo[:, 2 * j:2 * j + 2, :], mixf[:, :].rearrange("p (k t) -> p k t", k=2),
                                  yhi[:, 2 * j:2 * j + 2, :].bitcast(F32), ALU.subtract).then_inc(mix["lo"], 1)
            for j in range(3):
                lo(first["w3"] + j + RING)

            def post_norm(name, gain_in, src):
                k = NORM[name]
                dve.wait_ge(nrm["rs"], k + 1)
                dve.wait_ge(gain_in, 16)
                for t in range(TT):
                    last = dve.scalar_tensor_tensor(halves(xn, t), acc[:, :, t, :], rs[:, k, t:t + 1], gpost[:, :].rearrange("p (c n) -> p c n", c=2),
                                                    ALU.mult, ALU.mult)
                link(last)
                dve.sem_inc(dve_emptied, 1)
                for t in range(TT):
                    dve.tensor_tensor(h[:, t, :], h[:, t, :], xn[:, t, :], ALU.add).then_inc(nrm["src"], 1)
                dve.wait_ge(nrm["src"], src)

            dve.wait_ge(fil["t"], FILL["a"][0] + 4)
            post_norm("mix", gpost_in, SRC["h4"] + 2)
            norm_rows("h4")
            lo(first["w3"] + 3 + RING)
            fill("h4", xhi, xlo, C["norm_ffn_pre_2"])

            n0 = first["cv"]

            def conv_taps(b, j, k):
                dve.wait_ge(cvs["base"], k)
                for g in range(2):
                    c = C["conv_w_2"] + 44 + g * NT2
                    last = dve.scalar_tensor_tensor(cy[:, b, g, 1:], tb[:, b, g * T:g * T + T - 1],
                                                    cols[:, bass.ds(j + c, 1)], cy[:, b, g, 1:], ALU.mult, ALU.add)
                last.then_inc(cvs["tap1"], 1)
                dve.wait_ge(cvs["tap1"], k)
                for g in range(2):
                    c = C["conv_w_2"] + g * NT2
                    last = dve.scalar_tensor_tensor(cy[:, b, g, 2:], tb[:, b, g * T:g * T + T - 2],
                                                    cols[:, bass.ds(j + c, 1)], cy[:, b, g, 2:], ALU.mult, ALU.add)
                last.then_inc(cvs["y"], 1)

            def conv_product(b, k):
                dve.wait_ge(cvs["gelu"], k)
                dve.tensor_tensor(cf[:, :], cg[:, :], cy[:, b, 1, :], ALU.mult).then_inc(cvs["f"], 1)

            def conv_lo(j, k):
                dve.wait_ge(cvs["hi"], k)
                s = bass.ds(j, 1)
                dve.tensor_tensor(vlo[:, s, :], cf[:, :].rearrange("p (a t) -> p a t", a=1), vhi[:, s, :].bitcast(F32),
                                  ALU.subtract).then_inc(cvs["lo"], 1)
                dve.wait_ge(cvs["lo"], k)

            conv_taps(0, 0, 1)
            dve.wait_ge(cvs["y"], 1)
            dve.sem_inc(dve_emptied, 1)
            lo(n0 + RING)
            with dve.Fori(0, 7) as i:
                for u in range(RING):
                    conv_taps((u + 1) % RING, i * RING + (u + 1), i * RING + (u + 2))
                    conv_product(u, i * RING + (u + 1))
                    dve.wait_ge(cvs["y"], i * RING + (u + 2))
                    dve.sem_inc(dve_emptied, 1)
                    loop_lo(i, n0 + u + 1 + RING)
                    conv_lo(i * RING + u, i * RING + (u + 1))
            conv_product(0, 22)
            conv_lo(21, 22)
            for j in range(NT2 // 2):
                lo(first["wd"] + j + RING)
            post_norm("end", gpost2_in, SRC["end"] + 2)


NAMES = ["x", "mem", "norm_mix_g", "w_in", "fox_f_bias", "hgrn_lb_logits", "hgrn_norm_g", "w_out", "norm_x_g",
         "norm_mem_g", "w_xq", "w_xkv", "w_xo", "norm_ff_g", "w1", "w2", "final_norm_g", "mem_2", "norm_mix_pre_2",
         "w_in_2", "lambda_q1_2", "lambda_k1_2", "lambda_q2_2", "lambda_k2_2", "subln_g_2", "w_attn_branch_2",
         "pool_w_2", "pool_scale_2", "w_pool_branch_2", "norm_mem_2", "w_mem_kv_2", "w_mem_branch_2", "w_out_2",
         "norm_mix_post_2", "norm_ffn_pre_2", "w_up_2", "conv_w_2", "conv_b_2", "w_down_2", "norm_ffn_post_2"]


def kernel(**inputs):
    import numpy as np
    import concourse.bacc as bacc
    from concourse import mybir as _mybir
    from concourse.bass_utils import run_bass_kernel_spmd

    nc = bacc.Bacc("TRN2", target_bir_lowering=False, num_devices=1)
    arrays, w = {}, {}
    for name in NAMES:
        a = np.ascontiguousarray(inputs[name])
        arrays[f"in_{name}"] = a
        w[name] = nc.dram_tensor(f"in_{name}", a.shape, _mybir.dt.from_np(a.dtype), kind="ExternalInput").ap()
    out = nc.dram_tensor("out_0", (1, T, D), _mybir.dt.float32, kind="ExternalOutput").ap()
    two_blocks(nc, w, out)
    return run_bass_kernel_spmd(nc, [arrays], core_ids=[0]).results[0]["out_0"]
```

```python
from contextlib import ExitStack

import concourse.bass as bass
from concourse import mybir

F32 = mybir.dt.float32
F32R = mybir.dt.float32r
U32 = mybir.dt.uint32
BF16 = mybir.dt.bfloat16
ALU = mybir.AluOpType
ACT = mybir.ActivationFunctionType
AX = mybir.AxisListType.X

P = 128
D = 1024
KT = D // P
T = 256
TT = T // P
FOX = 512
FOX_H = 8
HG_H = 4
FF1 = 4096
FF2 = 2816
NT2 = FF2 // P
RING = 3
SLAB = 2048
NEG = -1e30
EPS = 1e-6
LN_MIN = 2.0 ** -64
LAM_INIT = 0.2
ALIBI = [2.0 ** -(h + 1) for h in range(8)]
POOL_W = (2, 4, 8, 16)
PAD = 16


def plan(w):
    slabs, first = [], {}

    def cols(name, wt, c0, n, nk=8, c=256, evac="act", k0=0):
        first[name] = len(slabs)
        for j in range(n):
            ap = wt[k0 * P:(k0 + nk) * P, c0 + j * c:c0 + (j + 1) * c].rearrange("(k p) c -> p k c", p=P)
            slabs.append(("T", ap, nk, c, evac))

    def half(name, wt, c0, n, evac="act"):
        first[name] = len(slabs)
        for j in range(n):
            for k in range(2):
                ap = wt[k * 512:(k + 1) * 512, c0 + j * 512:c0 + (j + 1) * 512].rearrange("(k p) c -> p k c", p=P)
                slabs.append(("N", ap, 4, 512, evac if k else None))

    def rows(name, wt, n, evac="dve"):
        first[name] = len(slabs)
        for j in range(n):
            ap = wt[j * 256:(j + 1) * 256, :].rearrange("(k p) c -> p k c", p=P)
            slabs.append(("N", ap, 2, 1024, evac if j == n - 1 else None))

    wi = w["w_in"]
    cols("gf", wi, 2056, 2, evac="act")
    cols("gq", wi, 1544, 2, evac="dve")
    cols("ff", wi, 1536, 1, c=128, evac="dve")
    cols("fq", wi, 0, 2)
    cols("fk", wi, 512, 2)
    half("fv", wi, 1024, 1)
    half("gi", wi, 2568, 1)
    half("gg", wi, 3080, 1, evac="dve")
    cols("xk", w["w_xkv"], 0, 4)
    half("xv", w["w_xkv"], D, 2)
    cols("km", w["w_mem_kv_2"], 0, 2)
    half("vm", w["w_mem_kv_2"], 512, 1)
    rows("wo", w["w_out"], 4)
    cols("xq", w["w_xq"], 0, 4)
    rows("xo", w["w_xo"], 4)
    cols("w1", w["w1"], 0, 16)
    rows("w2", w["w2"], 16)
    wi = w["w_in_2"]
    cols("qd", wi, 0, 4)
    cols("kd", wi, 1024, 4)
    rows("vd", wi[:, 2048:3072], 4, evac="act")
    cols("up", wi, 3072, 2)
    cols("qm", wi, 3584, 2)
    cols("ga", wi, 4096, 12)
    cols("pb", w["w_pool_branch_2"], 0, 2, nk=4, c=512, evac="dve")
    cols("mb", w["w_mem_branch_2"], 0, 2, nk=4, c=512, evac="dve")
    cols("ab", w["w_attn_branch_2"], 0, 4, evac="dve")
    rows("w3", w["w_out_2"], 4)
    first["cv"] = len(slabs)
    for j in range(NT2):
        ap = w["w_up_2"].rearrange("(k p) (two c) -> p k two c", p=P, two=2)[:, :, :, j * P:(j + 1) * P]
        slabs.append(("T", ap, 8, 256, "dve"))
    rows("wd", w["w_down_2"], NT2 // 2)
    return slabs, first


def two_blocks(nc, w, out):
    w = dict(w)
    for k in ("x", "mem", "mem_2", "w_in", "w_out", "w_xq", "w_xkv", "w_xo", "w1", "w2", "w_in_2", "w_attn_branch_2",
              "w_pool_branch_2", "w_mem_kv_2", "w_mem_branch_2", "w_out_2", "w_up_2", "w_down_2"):
        w[k] = w[k][0]
    slabs, first = plan(w)
    NS = len(slabs)
    act_evacs, dve_evacs, a, d = [], [], 0, 0
    for s in slabs:
        a, d = a + (s[4] == "act"), d + (s[4] == "dve")
        act_evacs.append(a)
        dve_evacs.append(d)

    landed = [0] * NS
    for n in range(NS):
        landed[n] = (landed[n - RING] if n >= RING else 0) + (16 if n < first["cv"] else 32)

    with ExitStack() as ctx:
        def sem(name):
            return ctx.enter_context(nc.semaphore(name))

        def sb(name, shape, dt=F32, at=None):
            return (at or ctx).enter_context(nc.sbuf_tensor(name, shape, dt))

        def sems(prefix, names):
            return {n: sem(f"{prefix}_{n}") for n in names.split()}

        raw = sb("raw", [P, RING, SLAB])
        whi = sb("whi", [P, RING, SLAB], F32R)
        wlo = sb("wlo", [P, RING, SLAB], F32R)
        xhi = sb("xhi", [P, KT, T], F32R)
        xlo = sb("xlo", [P, KT, T], F32R)
        h = sb("h", [P, TT, D])
        xn = sb("xn", [P, TT, D])
        junk = sb("junk", [P, 512], BF16)
        kmT = sb("kmT", [P, 4, T])
        vm = sb("vm", [P, TT, 512])
        ident = sb("ident", [P, P])
        cols = sb("cols", [P, 256])
        negF = sb("negF", [P, T])
        dg = sb("dg", [P, TT, P])
        ss = sb("ss", [P, 10, 2, 2])
        rs = sb("rs", [P, 10, 2])
        half_neg = sb("half_neg", [P, 16])
        small = sb("small", [P, 64])
        mx = sb("mx", [P, 4, 4])
        nmx = sb("nmx", [P, 4, 4])
        den = sb("den", [P, 4, 4])
        rden = sb("rden", [P, 4, 4])

        with ExitStack() as st:
            xkT = sb("xkT", [P, KT, T], at=st)
            xv = sb("xv", [P, TT, D], at=st)
            with ExitStack() as r1:
                fqT = sb("fqT", [P, 4, T], at=r1)
                fkT = sb("fkT", [P, 4, T], at=r1)
                fv = sb("fv", [P, TT, FOX], at=r1)
                gi = sb("gi", [P, TT, FOX], at=r1)
                gg = sb("gg", [P, TT, FOX], at=r1)
                qs = sb("qs", [P, HG_H * T], at=r1)
                kk = sb("kk", [P, HG_H * T], at=r1)
                bb = sb("bb", [P, HG_H * T], at=r1)
                dz = sb("dz", [P, 2, HG_H * T], at=r1)
                am = sb("am", [P, 12, P], at=r1)
                fs = sb("fs", [P, 2, 384], at=r1)
                fpt = sb("fpt", [P, 2, 384], at=r1)
                mhi = sb("mhi", [P, KT, T], F32R, at=r1)
                mlo = sb("mlo", [P, KT, T], F32R, at=r1)
                lvl = sb("lvl", [P, 7, P], at=r1)
                causal = sb("causal", [P, 384], at=r1)
            with ExitStack() as r2:
                xqT = sb("xqT", [P, KT, T], at=r2)
                cs = sb("cs", [P, 4, 512], at=r2)
                cpt = sb("cpt", [P, 2, 512], at=r2)
                chi = sb("chi", [P, KT, T], F32R, at=r2)
                clo = sb("clo", [P, KT, T], F32R, at=r2)
        with ExitStack() as r3:
            hid_hi = sb("hid_hi", [P, FF1 // P, T], F32R, at=r3)
            hid_lo = sb("hid_lo", [P, FF1 // P, T], F32R, at=r3)
            ru = sb("ru", [P, 512], at=r3)
            sq = sb("sq", [P, 512], at=r3)
            gbc = sb("gbc", [P, D], at=r3)
        with ExitStack() as r4:
            qdT = sb("qdT", [P, KT, T], at=r4)
            kdT = sb("kdT", [P, KT, T], at=r4)
            vd = sb("vd", [P, TT, D], at=r4)
            upad = sb("upad", [P, 4, PAD + T], at=r4)
            uw = sb("uw", [P, 2, PAD + T], at=r4)
            qmT = sb("qmT", [P, 4, T], at=r4)
            gates = sb("gates", [P, 24, T], at=r4)
            phi = sb("phi", [P, 4, T], F32R, at=r4)
            plo = sb("plo", [P, 4, T], F32R, at=r4)
            ohi = sb("ohi", [P, 4, T], F32R, at=r4)
            olo = sb("olo", [P, 4, T], F32R, at=r4)
            ndist = sb("ndist", [P, 384], at=r4)
            ds_ = sb("ds_", [P, 2, 384], at=r4)
            dpt = sb("dpt", [P, 384], at=r4)
            ms = sb("ms", [P, 512], at=r4)
            mpt = sb("mpt", [P, 512], at=r4)
            pw = sb("pw", [P, 4, P], at=r4)
            rcnt = sb("rcnt", [P, PAD], at=r4)
        with ExitStack() as r5:
            gpost = sb("gpost", [P, D], at=r5)
            yhi = sb("yhi", [P, KT, T], F32R, at=r5)
            ylo = sb("ylo", [P, KT, T], F32R, at=r5)
            mixf = sb("mixf", [P, 512], at=r5)
            vhi = sb("vhi", [P, NT2, T], F32R, at=r5)
            vlo = sb("vlo", [P, NT2, T], F32R, at=r5)
            cy = sb("cy", [P, RING, 2, T], at=r5)
            cg = sb("cg", [P, T], at=r5)
            cf = sb("cf", [P, T], at=r5)

        tb = ctx.enter_context(nc.psum_tensor("tb", [P, 4, 512], F32))
        acc = ctx.enter_context(nc.psum_tensor("acc", [P, 2, TT, 512], F32))

        names = ["norm_mix_g", "norm_x_g", "norm_mem_g", "norm_ff_g", "norm_mix_pre_2", "norm_mem_2", "norm_ffn_pre_2"]
        C = {n: 8 * i + (8 if i else 0) for i, n in enumerate(names)}
        C["pool_scale_2"], C["lb"], C["hgrn_norm_g"], C["subln_g_2"], C["conv_b_2"] = 64, 8, 68, 69, 70
        C["conv_w_2"] = 114
        NC0, NCW = 114, 132

        raw_landed = [sem(f"raw_landed{i}") for i in range(RING)]
        hi_ready, lo_ready, slab_done = sem("hi_ready"), sem("lo_ready"), sem("slab_done")
        act_emptied, dve_emptied = sem("act_emptied"), sem("dve_emptied")
        x_in = [sem(f"x_in{q}") for q in range(4)]
        first_rows_in, first_half_hi, first_half_lo = sem("first_rows_in"), sem("first_half_hi"), sem("first_half_lo")
        rows_in, lam_in, bias_in, mem_in, mem2_in = (sem(n) for n in "rows_in lam_in bias_in mem_in mem2_in".split())
        pw_in, gfin_in, gpost_in, gpost2_in, stored = (sem(n) for n in "pw_in gfin_in gpost_in gpost2_in stored".split())
        act_link, dve_link, pool_link = sem("act_link"), sem("dve_link"), sem("pool_link")
        consts_ready, cols_t, cols_ready, lam_ready, lb_ready = (
            sem(n) for n in "consts_ready cols_t cols_ready lam_ready lb_ready".split())
        nrm = sems("nrm", "src ss rs dg")
        part_done = sem("part_done")
        fil = sems("fil", "t hi lo")
        hg = sems("hg", "ln sq qs d e z prod merged out sq2 ss rs rec rd gsig gg kk")
        fx = sems("fx", "z l F")
        fox = sems("fox", "scores read max exp p pt ptc pv pvhi pvlo")
        cr = sems("cr", "scores max exp p pt ptc pv pvhi pvlo")
        df = sems("df", "scores read max exp p pt ptc pv o")
        me = sems("me", "scores max exp p pt ptc pv pvhi pvlo")
        ffn = sems("ffn", "sq hi lo")
        pl = sems("pl", "ready mm hi lo")
        lamx, oss, ors, gx, gates_ready, h_ready, post_made = (
            sem(n) for n in "lamx oss ors gx gates_ready h_ready post_made".split())
        mix = sems("mix", "f hi lo")
        cvs = sems("cvs", "base tap1 y gelu f hi lo")

        FILL, g0 = {}, 0
        BY_TILE = ("h1", "h2", "x2", "h4")
        for name, n in (("x", 4), ("mem", 4), ("mem2", 4), ("rec", 2), ("h1", 8), ("h2", 8), ("x2", 8), ("a", 4), ("h4", 8)):
            FILL[name] = (g0, n)
            g0 += n
        NORM = {n: i for i, n in enumerate(["x", "mem", "mem2", "h1", "h2", "h3", "x2", "mix", "h4", "end"])}
        SRC = {n: 4 * i for i, n in enumerate(["h1", "h2", "h3", "x2", "h4", "end"])}
        SS = {n: 4 * i for i, n in enumerate(["x", "mem", "mem2", "h1", "h2", "h3", None, "mix", "h4", "end"])}
        RS = {n: 2 * i for i, n in enumerate(["x", "mem", "mem2", "h1", "h2", "h3", "mix", "h4", "end"])}
        DG = {n: 2 * i for i, n in enumerate(["x", "mem", "mem2", "h1", "h2", "x2", "h4"])}
        lasts = [first["wo"] + 3, first["xo"] + 3, first["w2"] + 15, first["w3"] + 3, NS - 1]
        PARTS = {n: 3 * i for i, n in enumerate(lasts)}
        QUARTERS = [(t, c) for t in range(TT) for c in range(2)]

        def fill_banks(n):
            return [n % 2, 2, 3, 1 - n % 2]

        BANKS = {"x": fill_banks(0), "mem": [2, 3, 6, 7], "mem2": [first["km"] % 2, 1 - first["km"] % 2, 4, 5], "rec": [2, 3],
                 "h1": fill_banks(first["xq"]), "h2": fill_banks(0), "x2": fill_banks(first["qd"]), "a": [4, 6, 5, 7],
                 "h4": fill_banks(0)}

        def src_count(name, q):
            return SRC["h3"] + 2 * q + 1 + (name == "x2") if name in ("h3", "x2") else SRC[name] + q + 1

        def wait_quarter(engine, n, q):
            if q < 3:
                engine.wait_ge(part_done, PARTS[n] + q + 1)
            else:
                engine.wait_ge(slab_done, n + 1)

        LEVELS = 9

        def slab(t, n, nk):
            return t[:, n % RING, :nk * slabs[n][3]].rearrange("p (k c) -> p k c", k=nk)

        def fill_steps(name):
            g0, n = FILL[name]
            if name not in BY_TILE:
                return [(g0 + g + 1, g, slice(0, T)) for g in range(n)]
            return [(g0 + 4 * t + g + 1, g, slice(t * P, t * P + P)) for t in range(TT) for g in range(4)]

        def fill_bank(name, g):
            b = BANKS[name][g % len(BANKS[name])]
            return tb[:, b, :] if b < 4 else acc[:, (b - 4) // 2, b % 2, :]

        def cross_bank(i):
            return acc[:, 0, i, :] if i < 2 else tb[:, i, :]

        def cross_pt_bank(i):
            return acc[:, 1, i, :] if i < 2 else tb[:, (first["xq"] + i) % 2, :]

        def quarter(t, q):
            tt, c = QUARTERS[q]
            return t[:, tt, c * 512:c * 512 + 512]

        def lvl_view(t, m):
            half = 1 << (m - 1)
            return t.rearrange("p (g r u) -> p g r u", r=2, u=half)

        block = ctx.enter_context(nc.Block())

        @block.sync
        def _(sp):
            def load(n, src=None, wait=None):
                if n >= RING:
                    sp.wait_ge(lo_ready, n - RING + 1 if wait is None else wait)
                _, ap, nk, c, _ = slabs[n]
                dst, src = slab(raw, n, nk), ap if src is None else src
                if n < first["cv"]:
                    sp.dma_start(dst, src).then_inc(raw_landed[n % RING], 16)
                    return
                for part in range(2):
                    if len(src.shape) == 4:
                        d, s = dst[:, :, part * P:part * P + P], src[:, :, part, :]
                    else:
                        d, s = dst[:, part, :], src[:, part, :]
                    sp.dma_start(d, s).then_inc(raw_landed[n % RING], 16)

            def loop(name, src, iters):
                n0 = first[name]
                with sp.Fori(0, iters) as i:
                    for u in range(RING):
                        load(n0 + u, src(i, u), i * RING + (n0 + u - RING + 1))

            for q, (t, c) in enumerate(QUARTERS):
                sp.dma_start(quarter(h, q), w["x"][t * P:t * P + P, c * 512:c * 512 + 512]).then_inc(x_in[q], 16)
            for n in range(RING):
                load(n)
            for n in names[1:]:
                sp.dma_start(fs[C[n]:C[n] + 8, 0, 0:P], w[n].rearrange("a (k p) -> (a k) p", p=P)).then_inc(rows_in, 16)
            sp.dma_start(fs[64:68, 0, 0:P], w["pool_scale_2"].rearrange("a (k p) -> (a k) p", p=P)).then_inc(rows_in, 16)
            sp.dma_start(fs[68:69, 0, 0:P], w["hgrn_norm_g"]).then_inc(rows_in, 16)
            sp.dma_start(fs[69:70, 0, 0:P], w["subln_g_2"]).then_inc(rows_in, 16)
            sp.dma_start(fs[70:114, 0, 0:P], w["conv_b_2"].rearrange("a (k p) -> (a k) p", p=P)).then_inc(rows_in, 16)
            cw = w["conv_w_2"].rearrange("a j (k p) -> (a j k) p", p=P)
            sp.dma_start(fs[0:66, 0, P:T], cw[0:66, :]).then_inc(rows_in, 16)
            sp.dma_start(fs[0:66, 0, T:384], cw[66:132, :]).then_inc(rows_in, 16)
            sp.dma_start(small[0:8, 59:60], w["fox_f_bias"].rearrange("a h -> h a"),
                         allow_slow_non_contiguous=True).then_inc(bias_in, 16)
            for i, n in enumerate(("lambda_q1_2", "lambda_k1_2", "lambda_q2_2", "lambda_k2_2")):
                sp.dma_start(fpt[:, 0, 64 * i:64 * i + 64], w[n].broadcast_to([P, 64])).then_inc(lam_in, 16)
            for n in range(RING, first["w1"]):
                load(n)
            w1v = w["w1"].rearrange("(k p) c -> p k c", p=P)
            loop("w1", lambda i, u: w1v[:, :, bass.ds(i * 768 + u * 256, 256)], 5)
            load(first["w1"] + 15)
            w2v = w["w2"].rearrange("(j k p) c -> p j k c", p=P, k=2)
            loop("w2", lambda i, u: w2v[:, bass.ds(i * 3 + u, 1), :, :].rearrange("p j k c -> p (j k) c"), 5)
            load(first["w2"] + 15)
            for n in range(first["qd"], first["cv"]):
                load(n)
            upv = w["w_up_2"].rearrange("(k p) (two c) -> p k two c", p=P, two=2)
            loop("cv", lambda i, u: upv[:, :, :, bass.ds(i * 384 + u * 128, 128)], 7)
            for n in range(first["cv"] + 21, NS):
                load(n)

        @block.gpsimd
        def _(pool):
            count = [0]

            def link(ins):
                count[0] += 1
                ins.then_inc(pool_link, 1)
                pool.wait_ge(pool_link, count[0])

            def select(t, pattern, base, chan, op, fill):
                link(pool.affine_select(out=t, in_=t, compare_op=op, fill=fill, base=base, pattern=pattern,
                                        channel_multiplier=chan))

            pool.memset(half_neg[:, :], -0.5)
            pool.memset(negF[:, :], 0.0)
            pool.memset(lvl[:, :, :], 0.0)
            pool.memset(causal[:, :], 0.0)
            link(pool.memset(ident[:, :], 0.0))
            select(ident[:, :], [[-1, P]], 0, 1, ALU.not_equal, 1.0)
            select(causal[:, 0:P], [[-1, P]], 0, 1, ALU.is_ge, NEG)
            select(causal[:, 256:384], [[-1, P]], 0, 1, ALU.is_ge, NEG)
            pool.sem_inc(consts_ready, 1)

            def diagonal(name, t):
                if DG[name] and t == 0:
                    pool.wait_ge(fil["t"], sum(FILL[[m for m in DG if DG[m] == DG[name] - 2][0]]))
                k = NORM[name]
                pool.wait_ge(nrm["rs"], RS["h3" if name == "x2" else name] + t + 1)
                pool.tensor_scalar(dg[:, t, :], ident[:, :], rs[:, k, t:t + 1], None, ALU.mult).then_inc(nrm["dg"], 1)

            def rms(name):
                k = NORM[name]
                for t in range(TT):
                    pool.wait_ge(nrm["ss"], SS[name] + 2 * t + 2)
                    link(pool.tensor_scalar(rs[:, k, t:t + 1], ss[:, k, t, 0:1], ss[:, k, t, 1:2], EPS, ALU.add, ALU.add))
                    pool.tensor_tensor(rs[:, k, t:t + 1], rs[:, k, t:t + 1], half_neg[:, 0:1], ALU.pow).then_inc(nrm["rs"], 1)
                    if name in DG:
                        diagonal(name, t)

            def rms_twice(name):
                k = NORM[name]
                for t in range(TT):
                    pool.wait_ge(nrm["ss"], SS[name] + 4 * t + 4)
                    m, both = rs[:, k, t:t + 1], rs[:, k + 1, t:t + 1]
                    pool.tensor_tensor(both, ss[:, k + 1, t, 0:1], ss[:, k + 1, t, 1:2], ALU.add)
                    link(pool.tensor_scalar(m, ss[:, k, t, 0:1], ss[:, k, t, 1:2], EPS, ALU.add, ALU.add))
                    link(pool.tensor_scalar(both, m, EPS, both, ALU.mult, ALU.add))
                    pool.tensor_tensor(rs[:, k:k + 2, t], rs[:, k:k + 2, t], half_neg[:, 0:2], ALU.pow).then_inc(nrm["rs"], 1)
                    diagonal("x2", t)

            rms("x")
            for m in range(1, 8):
                half = 1 << (m - 1)
                n = P // (2 * half)
                t = lvl[:, m - 1, :].rearrange("p (g r u) -> p g r u", r=2, u=half)[:, :, 1, :]
                link(pool.memset(t, 1.0))
                select(t, [[-2 * half, n], [0, half]], 0, 1, ALU.is_ge, 0.0)
                select(t, [[2 * half, n], [0, half]], half - 1, -1, ALU.is_ge, 0.0)
            pool.sem_inc(consts_ready, 1)
            pool.wait_ge(fil["t"], FILL["x"][0] + 4)
            pool.dma_start(xn[:, :, :], w["mem"].rearrange("(t p) c -> p t c", p=P)).then_inc(mem_in, 16)
            rms("mem")
            pool.wait_ge(fil["t"], FILL["mem"][0] + 4)
            pool.dma_start(xn[:, :, :], w["mem_2"].rearrange("(t p) c -> p t c", p=P)).then_inc(mem2_in, 16)
            rms("mem2")

            pool.wait_ge(hg["kk"], 2)
            pool.wait_ge(hg["qs"], 2)
            for m in range(1, LEVELS):
                pool.wait_ge(hg["e"], m)
                z = lvl_view(dz[:, m % 2, :], m)
                pool.tensor_tensor(z[:, :, 0, :], z[:, :, 0, :], lvl_view(kk[:, :], m)[:, :, 0, :], ALU.mult)
                pool.tensor_tensor(z[:, :, 1, :], z[:, :, 1, :], lvl_view(qs[:, :], m)[:, :, 1, :], ALU.mult)\
                    .then_inc(hg["z"], 1)
            pool.wait_ge(hg["ss"], 1)
            link(pool.tensor_scalar(small[:, 8:16], small[:, 0:8], 1.0 / P, EPS, ALU.mult, ALU.add))
            pool.tensor_tensor(small[:, 8:16], small[:, 8:16], half_neg[:, 0:8], ALU.pow).then_inc(hg["rs"], 1)
            rms("h1")
            rms("h2")
            pool.dma_start(gbc[:, :], w["final_norm_g"].rearrange("(a c) -> a c", a=1).broadcast_to([P, D])
                           ).then_inc(gfin_in, 16)
            rms_twice("h3")
            pool.dma_start(pw[:, :, :], w["pool_w_2"][0].rearrange("g c d -> c g d")).then_inc(pw_in, 16)
            pool.memset(upad[:, :, 0:PAD], 0.0)
            pool.memset(uw[:, :, 0:PAD], 0.0)
            for c0, base in ((0, 0), (P, P), (2 * P, 0)):
                pool.iota(ndist[:, c0:c0 + P], [[1, P]], base=-base, channel_multiplier=-1,
                          allow_small_or_imprecise_dtypes=True)
            link(pool.iota(rcnt[:, :], [[1, PAD]], base=1, channel_multiplier=0, allow_small_or_imprecise_dtypes=True))
            select(ndist[:, 0:P], [[-1, P]], 0, 1, ALU.is_ge, NEG)
            select(ndist[:, 256:384], [[-1, P]], 0, 1, ALU.is_ge, NEG)
            link(pool.tensor_tensor(rcnt[:, :], rcnt[:, :], half_neg[:, :], ALU.pow))
            link(pool.tensor_tensor(rcnt[:, :], rcnt[:, :], rcnt[:, :], ALU.mult))
            pool.sem_inc(consts_ready, 1)
            pool.wait_ge(act_emptied, act_evacs[first["up"] + 1])
            for g, win in enumerate(POOL_W):
                src, width, b = upad[:, g, :], 1, 0
                while width < win:
                    dst = uw[:, b, :]
                    link(pool.tensor_tensor(dst[:, PAD:], src[:, PAD:], src[:, PAD - width:PAD + T - width], ALU.add))
                    src, width, b = dst, 2 * width, 1 - b
                n = win - 1
                dst = uw[:, b, :]
                pool.tensor_scalar(dst[:, PAD + n:], src[:, PAD + n:], 1.0 / win, 0.0, ALU.mult, ALU.add)
                link(pool.tensor_tensor(dst[:, PAD:PAD + n], src[:, PAD:PAD + n], rcnt[:, 0:n], ALU.mult))
                link(pool.tensor_tensor(upad[:, g, PAD:], dst[:, PAD:], upad[:, g, PAD:], ALU.subtract))
            pool.sem_inc(pl["ready"], 1)
            pool.wait_ge(oss, 1)
            link(pool.tensor_scalar(small[:, 32:48], small[:, 16:32], 1.0 / P, EPS, ALU.mult, ALU.add))
            pool.tensor_tensor(small[:, 32:48], small[:, 32:48], half_neg[:, :], ALU.pow).then_inc(ors, 1)
            pool.wait_ge(df["scores"], 8)
            pool.dma_start(gpost[:, :], w["norm_mix_post_2"].broadcast_to([P, D])).then_inc(gpost_in, 16)
            rms("mix")
            rms("h4")
            pool.dma_start(gpost[:, :], w["norm_ffn_post_2"].broadcast_to([P, D])).then_inc(gpost2_in, 16)
            rms("end")

        @block.tensor
        def _(pe):
            def mm3(o, a_hi, a_lo, b_hi, b_lo, start, stop):
                pe.matmul(o, a_hi, b_hi, start=start, stop=False)
                pe.matmul(o, a_hi, b_lo, start=False, stop=False)
                return pe.matmul(o, a_lo, b_hi, start=False, stop=stop)

            def split_ready(n, value=None):
                pe.wait_ge(hi_ready, n + 1 if value is None else value)
                pe.wait_ge(lo_ready, n + 1 if value is None else value)

            def emptied(n):
                if slabs[n][4] == "act":
                    pe.wait_ge(act_emptied, act_evacs[n])
                else:
                    pe.wait_ge(dve_emptied, dve_evacs[n])

            def t_slab(n, hi, lo, bank, value=None, fresh=None):
                split_ready(n, value)
                nk = slabs[n][2]
                a_hi, a_lo = slab(whi, n, nk), slab(wlo, n, nk)
                for c in range(slabs[n][3] // P):
                    o = tb[:, bank + c // 2, (c % 2) * T:(c % 2) * T + T]
                    for k in range(nk):
                        if fresh and c == 0 and k % 2 == 0:
                            pe.wait_ge(fil["lo"], sum(FILL[fresh]) - 3 + k // 2)
                        last = mm3(o, a_hi[:, k, c * P:(c + 1) * P], a_lo[:, k, c * P:(c + 1) * P],
                                   hi[:, k, :], lo[:, k, :], k == 0, k == nk - 1)
                last.then_inc(slab_done, 1)

            def half_slab(n, hi, lo, k0, pair):
                split_ready(n)
                b_hi, b_lo = slab(whi, n, 4), slab(wlo, n, 4)
                for t in range(TT):
                    o = acc[:, pair, t, :]
                    for k in range(4):
                        a = (k0 + k, slice(t * P, t * P + P))
                        last = mm3(o, hi[:, a[0], a[1]], lo[:, a[0], a[1]], b_hi[:, k, :], b_lo[:, k, :],
                                   k0 + k == 0, k0 + k == 7)
                last.then_inc(slab_done, 1)

            def row_slab(n, hi, lo, k0, nk_all):
                split_ready(n)
                b_hi, b_lo = slab(whi, n, 2), slab(wlo, n, 2)
                for t in range(TT):
                    for c in range(2):
                        o = acc[:, c, t, :]
                        for k in range(2):
                            a = slice(t * P, t * P + P)
                            last = mm3(o, hi[:, k0 + k, a], lo[:, k0 + k, a], b_hi[:, k, c * 512:c * 512 + 512],
                                       b_lo[:, k, c * 512:c * 512 + 512], k0 + k == 0, k0 + k == nk_all - 1)
                        if n in PARTS and (t, c) != (1, 1):
                            last.then_inc(part_done, 1)
                last.then_inc(slab_done, 1)

            def fill_rows(name, src):
                for count, g, _ in fill_steps(name):
                    if g >= len(BANKS[name]):
                        pe.wait_ge(fil["lo"], count - len(BANKS[name]))
                    o = fill_bank(name, g)
                    for k in range(2):
                        for t in range(TT):
                            last = pe.transpose(o[:, k * T + t * P:k * T + t * P + P],
                                                src[:, t, (g * 2 + k) * P:(g * 2 + k + 1) * P], ident[:, :])
                    last.then_inc(fil["t"], 1)

            def fill_norm(name, src):
                g0 = FILL[name][0]
                if g0:
                    pe.wait_ge(fil["lo"], g0)
                for t in range(TT):
                    pe.wait_ge(nrm["dg"], DG[name] + t + 1)
                    for g in range(4):
                        if name in BY_TILE and t:
                            pe.wait_ge(fil["lo"], g0 + g + 1)
                        for k in range(2):
                            f = 2 * g + k
                            last = pe.matmul(fill_bank(name, g)[:, k * T + t * P:k * T + t * P + P], src[:, t, f * P:f * P + P],
                                             dg[:, t, :], start=True, stop=True)
                        if name in BY_TILE or t:
                            last.then_inc(fil["t"], 1)

            def filled(name):
                g0, n = FILL[name]
                pe.wait_ge(fil["hi"], g0 + n)
                pe.wait_ge(fil["lo"], g0 + n)

            def keep_clock(n):
                for _ in range(n):
                    pe.transpose(tb[:, 3, 0:P], ident[:, :], ident[:, :])

            pe.wait_ge(consts_ready, 1)
            pe.wait_ge(first_rows_in, 32)
            pe.transpose(acc[:, 0, 0, 0:16], fs[0:16, 0, 0:P], ident[0:16, 0:16]).then_inc(cols_t, 1)
            for q in range(4):
                pe.wait_ge(x_in[q], 16)
            fill_norm("x", h)

            pe.wait_ge(first_half_lo, 1)
            A = first["gf"]
            for n in range(A, first["fv"]):
                if n >= 2:
                    emptied(n - 2)
                if n == 1:
                    filled("x")
                t_slab(n, xhi, xlo, n % 2, fresh=None if n else "x")
                if n == 1:
                    pe.wait_ge(rows_in, 16 * 12)
                    pe.transpose(acc[:, 0, 1, 0:NC0], fs[0:NC0, 0, 0:P], ident[0:NC0, 0:NC0])
                    for i in range(2):
                        last = pe.transpose(acc[:, 0, 1, NC0 + 66 * i:NC0 + 66 * i + 66], fs[0:66, 0, P * (i + 1):P * (i + 2)],
                                            ident[0:66, 0:66])
                    last.then_inc(cols_t, 1)
                if n == 4:
                    pe.wait_ge(mem_in, 16)
                    fill_norm("mem", xn)
            pe.wait_ge(cols_ready, 2)
            for j, name in enumerate(("fv", "gi", "gg")):
                if name == "gi":
                    pe.wait_ge(fil["lo"], FILL["mem"][0] + 4)
                elif name == "gg":
                    emptied(first["fv"] + 1)
                for k in range(2):
                    half_slab(first[name] + k, xhi, xlo, 4 * k, j % 2)

            def fox_scores(i):
                if i == 0:
                    emptied(first["fk"] + 1)
                    pe.wait_ge(fx["F"], 1)
                    pe.wait_ge(fil["lo"], FILL["mem"][0] + 4)
                pe.wait_ge(fox["read"], i) if i else None
                p0, c = (i % 2) * 64, i // 2
                for o, s, t in ((tb[:, 2, 0:P], P, 0), (tb[:, 2, P:384], T, 1)):
                    pe.matmul(o, ident[:, i:i + 1].broadcast_to([P, P]), negF[:, 0:s], start=True, stop=False)
                    last = pe.matmul(o, fqT[p0:p0 + 64, c, t * P:t * P + P], fkT[p0:p0 + 64, c, 0:s], start=False, stop=True)
                last.then_inc(fox["scores"], 1)

            def fox_transpose(i):
                pe.wait_ge(fox["p"], i + 1)
                if i:
                    pe.wait_ge(fox["pvlo"], i)
                for b in range(3):
                    last = pe.transpose(tb[:, 3, b * P:b * P + P], fs[:, i % 2, b * P:b * P + P], ident[:, :])
                last.then_inc(fox["pt"], 1)

            def fox_values(i):
                pe.wait_ge(fox["ptc"], i + 1)
                if i == 0:
                    emptied(first["fv"] + 1)
                p0 = (i % 2) * 64
                o, pt = tb[p0:p0 + 64, 3, :], fpt[:, i % 2, :]
                v = slice(i * 64, i * 64 + 64)
                pe.matmul(o[:, 0:P], fv[:, 0, v], pt[:, 0:P], start=True, stop=True)
                pe.matmul(o[:, P:T], fv[:, 0, v], pt[:, P:T], start=True, stop=False)
                pe.matmul(o[:, P:T], fv[:, 1, v], pt[:, T:384], start=False, stop=True).then_inc(fox["pv"], 1)

            def hg_products(m):
                if m == 0:
                    pe.wait_ge(hg["kk"], 2)
                    pe.wait_ge(hg["qs"], 2)
                    emptied(first["gi"] + 1)
                else:
                    pe.wait_ge(hg["z"], m)
                    pe.wait_ge(hg["merged"], m)
                z = dz[:, m % 2, :]
                a, b = (kk, qs) if m == 0 else (z, z)
                for i in range(HG_H):
                    if m == LEVELS - 1:
                        last = pe.matmul(acc[:, 1, 0, i * P:i * P + P], z[:, i * T:i * T + P],
                                         z[:, i * T + P:i * T + T], start=True, stop=True)
                        continue
                    for t in range(TT):
                        s = slice(i * T + t * P, i * T + t * P + P)
                        if m == 0:
                            last = pe.matmul(acc[:, 1, t, i * P:i * P + P], a[:, s], b[:, s], start=True, stop=True)
                        else:
                            last = pe.matmul(acc[:, 1, t, i * 64:i * 64 + 64], a[:, s], lvl_view(b[:, s], m)[:, :, 1, :],
                                             start=True, stop=True)
                last.then_inc(hg["prod"], 1)

            def hg_out():
                pe.wait_ge(hg["merged"], LEVELS)
                for i in range(HG_H):
                    v = slice(i * P, i * P + P)
                    pe.matmul(acc[:, 1, 0, v], am[:, i, :], gi[:, 0, v], start=True, stop=True)
                    pe.matmul(acc[:, 1, 1, v], am[:, 8 + i, :], gi[:, 0, v], start=True, stop=False)
                    last = pe.matmul(acc[:, 1, 1, v], am[:, 4 + i, :], gi[:, 1, v], start=False, stop=True)
                last.then_inc(hg["out"], 1)

            filled("mem")
            B = first["xk"]
            for i in range(12):
                n = B + i
                if i == 9:
                    filled("mem2")
                if n < first["xv"]:
                    emptied(n - 2 if i >= 2 else first["fk"] + i)
                    t_slab(n, mhi, mlo, n % 2)
                elif n < first["km"]:
                    if i == 4:
                        emptied(first["gg"] + 1)
                    elif i == 6:
                        emptied(first["xv"] + 1)
                    half_slab(n, mhi, mlo, 4 * (i % 2), 0)
                elif n < first["vm"]:
                    t_slab(n, mhi, mlo, n % 2, fresh="mem2" if i == 8 else None)
                else:
                    if i == 10:
                        emptied(first["xv"] + 3)
                    half_slab(n, mhi, mlo, 4 * (i % 2), 0)
                if i < 8:
                    if i:
                        fox_transpose(i - 1)
                    fox_scores(i)
                    if i == 7:
                        emptied(first["xk"] + 3)
                        emptied(first["xv"] + 3)
                        pe.wait_ge(mem2_in, 16)
                        fill_norm("mem2", xn)
                    hg_products(i)
                    if i:
                        fox_values(i - 1)
                elif i == 8:
                    fox_transpose(7)
                    hg_products(8)
                    fox_values(7)
                elif i == 9:
                    hg_out()
                elif i == 11:
                    pe.wait_ge(hg["rec"], 1)
                    fill_rows("rec", dz[:, 1, :].rearrange("p (t c) -> p t c", t=TT))

            emptied(first["vm"] + 1)
            pe.wait_ge(hg["rd"], 1)
            pe.wait_ge(fox["pvlo"], 8)
            for j in range(4):
                if j == 2:
                    filled("rec")
                row_slab(first["wo"] + j, xhi, xlo, 2 * j, 8)
            emptied(first["km"] + 1)
            fill_norm("h1", h)

            def cross_scores(i):
                emptied(first["xq"] + i)
                for t in range(TT):
                    o = cross_bank(i)[:, t * T:t * T + T]
                    for k in range(2):
                        last = pe.matmul(o, xqT[:, 2 * i + k, t * P:t * P + P], xkT[:, 2 * i + k, :], start=k == 0, stop=k == 1)
                last.then_inc(cr["scores"], 1)

            def cross_transpose(i):
                pe.wait_ge(cr["p"], i + 1)
                if i >= 2:
                    emptied(first["xq"] + i)
                for mt in range(TT):
                    for t in range(TT):
                        last = pe.transpose(cross_pt_bank(i)[:, mt * T + t * P:mt * T + t * P + P],
                                            cs[:, i, t * T + mt * P:t * T + mt * P + P], ident[:, :])
                last.then_inc(cr["pt"], 1)

            def cross_values(i):
                pe.wait_ge(cr["ptc"], i + 1)
                for dt in range(2):
                    for mt in range(TT):
                        last = pe.matmul(cross_bank(i)[:, dt * T:dt * T + T], xv[:, mt, i * T + dt * P:i * T + dt * P + P],
                                         cpt[:, i % 2, mt * T:mt * T + T], start=mt == 0, stop=mt == 1)
                last.then_inc(cr["pv"], 1)

            def cross_out(j):
                pe.wait_ge(cr["pvlo"], j + 1)
                row_slab(first["xo"] + j, chi, clo, 2 * j, 8)

            for j in range(4):
                n = first["xq"] + j
                if j >= 2:
                    emptied(n - 2)
                if j == 1:
                    filled("h1")
                t_slab(n, xhi, xlo, n % 2, fresh=None if j else "h1")
                if j == 1:
                    pe.wait_ge(dve_emptied, dve_evacs[first["wo"] + 3])
                    cross_scores(0)
                elif j == 2:
                    cross_scores(1)
                    cross_transpose(0)
            cross_values(0)
            cross_transpose(1)
            cross_scores(2)
            cross_values(1)
            cross_scores(3)
            pe.wait_ge(cr["pvlo"], 2)
            cross_out(0)
            cross_transpose(2)
            cross_transpose(3)
            cross_values(2)
            cross_values(3)
            cross_out(1)
            cross_out(2)
            cross_out(3)
            fill_norm("h2", h)

            def t_loop(name, iters, fresh):
                n0 = first[name]
                done = (act_emptied, act_evacs) if slabs[n0][4] == "act" else (dve_emptied, dve_evacs)
                with pe.Fori(0, iters) as i:
                    for u in range(RING):
                        pe.wait_ge(done[0], i * RING + (done[1][n0 + u] - RING))
                        if u == 1:
                            filled(fresh)
                        t_slab(n0 + u, xhi, xlo, u, i * RING + (n0 + u + 1), fresh=None if u else fresh)

            t_loop("w1", 5, "h2")
            n = first["w1"] + 15
            pe.wait_ge(act_emptied, act_evacs[n - RING])
            t_slab(n, xhi, xlo, 0)
            for j in range(16):
                pe.wait_ge(ffn["lo"], j + 1)
                row_slab(first["w2"] + j, hid_hi, hid_lo, 2 * j, 32)
            emptied(first["w1"] + 15)
            keep_clock(12)
            pe.wait_ge(nrm["src"], SRC["x2"] + 4)
            fill_norm("x2", xn)

            for n in range(first["qd"], first["vd"]):
                if n >= first["qd"] + 2:
                    emptied(n - 2)
                elif n == first["qd"] + 1:
                    filled("x2")
                t_slab(n, xhi, xlo, n % 2, fresh=None if n > first["qd"] else "x2")
            for j in range(4):
                if j == 0:
                    pe.wait_ge(dve_emptied, dve_evacs[first["w2"] + 15])
                row_slab(first["vd"] + j, xhi, xlo, 2 * j, 8)

            def diff_scores(i):
                if i == 0:
                    emptied(first["kd"] + 3)
                if i:
                    pe.wait_ge(df["read"], 2 * i)
                for c in range(2):
                    p0 = 64 * c
                    pe.matmul(tb[:, 2 + c, 0:P], qdT[p0:p0 + 64, i, 0:P], kdT[p0:p0 + 64, i, 0:P], start=True, stop=True)
                    last = pe.matmul(tb[:, 2 + c, P:384], qdT[p0:p0 + 64, i, P:T], kdT[p0:p0 + 64, i, 0:T],
                                     start=True, stop=True)
                last.then_inc(df["scores"], 1)

            def diff_transpose(i):
                pe.wait_ge(df["p"], i + 1)
                if i:
                    pe.wait_ge(df["ptc"], i)
                else:
                    emptied(first["vd"] + 3)
                for b in range(3):
                    last = pe.transpose(acc[:, 0, 0, b * P:b * P + P], ds_[:, 0, b * P:b * P + P], ident[:, :])
                last.then_inc(df["pt"], 1)

            def diff_values(i):
                pe.wait_ge(df["ptc"], i + 1)
                if i:
                    pe.wait_ge(df["o"], i)
                v = slice(i * P, i * P + P)
                pe.matmul(acc[:, 0, 1, 0:P], dpt[:, 0:P], vd[:, 0, v], start=True, stop=True)
                pe.matmul(acc[:, 0, 1, P:T], dpt[:, P:T], vd[:, 0, v], start=True, stop=False)
                pe.matmul(acc[:, 0, 1, P:T], dpt[:, T:384], vd[:, 1, v], start=False, stop=True).then_inc(df["pv"], 1)

            def mem_scores(i):
                if i:
                    pe.wait_ge(me["exp"], i)
                else:
                    emptied(first["qm"] + 1)
                for t in range(TT):
                    last = pe.matmul(acc[:, 1, 0, t * T:t * T + T], qmT[:, i, t * P:t * P + P], kmT[:, i, :], start=True, stop=True)
                last.then_inc(me["scores"], 1)

            def mem_transpose(i):
                pe.wait_ge(me["p"], i + 1)
                if i:
                    pe.wait_ge(me["ptc"], i)
                for mt in range(TT):
                    for t in range(TT):
                        last = pe.transpose(acc[:, 1, 1, mt * T + t * P:mt * T + t * P + P],
                                            ms[:, t * T + mt * P:t * T + mt * P + P], ident[:, :])
                last.then_inc(me["pt"], 1)

            def mem_values(i):
                pe.wait_ge(me["ptc"], i + 1)
                if i:
                    pe.wait_ge(me["pvlo"], i)
                for mt in range(TT):
                    last = pe.matmul(acc[:, 0, 1, 0:T], vm[:, mt, i * P:i * P + P], mpt[:, mt * T:mt * T + T],
                                     start=mt == 0, stop=mt == 1)
                last.then_inc(me["pv"], 1)

            for i in range(16):
                n = first["up"] + i
                emptied(n - 2 if i >= 2 else first["kd"] + 2 + i)
                t_slab(n, xhi, xlo, n % 2)
                if 1 <= i <= 8:
                    diff_transpose(i - 1)
                if i < 8:
                    diff_scores(i)
                elif i == 8:
                    mem_scores(0)
                if 1 <= i <= 8:
                    diff_values(i - 1)
                if 9 <= i <= 11:
                    mem_scores(i - 8)
                if i == 10:
                    pe.wait_ge(df["o"], 8)
                if 10 <= i <= 13:
                    mem_values(i - 10)
                if 9 <= i <= 12:
                    mem_transpose(i - 9)
                if i == 14:
                    pe.wait_ge(me["pvlo"], 4)
                    pe.wait_ge(pw_in, 16)
                    pe.wait_ge(pl["ready"], 1)
                    for g in range(4):
                        last = pe.matmul(acc[:, 0, g // 2, (g % 2) * T:(g % 2) * T + T], pw[:, g, :], upad[:, g, PAD:], start=True, stop=True)
                    last.then_inc(pl["mm"], 1)
            pe.wait_ge(pl["lo"], 1)
            pe.wait_ge(df["read"], 16)
            for j in range(2):
                if j:
                    emptied(first["ga"] + 10)
                    emptied(first["ga"] + 11)
                t_slab(first["pb"] + j, phi, plo, 2 - 2 * j)
            pe.wait_ge(gx, 1)
            fill_rows("a", xn)
            pe.wait_ge(me["pvlo"], 4)
            for j in range(2):
                emptied(first["pb"] + 1 - j)
                t_slab(first["mb"] + j, ohi, olo, 2 * j)
            filled("a")
            emptied(first["mb"])
            for j in range(4):
                if j >= 2:
                    emptied(first["ab"] + j - 2)
                t_slab(first["ab"] + j, xhi, xlo, j % 2)
            for j in range(4):
                pe.wait_ge(mix["lo"], j + 1)
                row_slab(first["w3"] + j, yhi, ylo, 2 * j, 8)
            emptied(first["ab"] + 3)
            keep_clock(28)
            fill_norm("h4", h)
            t_loop("cv", 7, "h4")
            n = first["cv"] + 21
            pe.wait_ge(dve_emptied, dve_evacs[n - RING])
            t_slab(n, xhi, xlo, 0)
            pe.wait_ge(dve_emptied, dve_evacs[first["w3"] + 3])
            for j in range(NT2 // 2):
                pe.wait_ge(cvs["lo"], 2 * j + 2)
                row_slab(first["wd"] + j, vhi, vlo, 2 * j, NT2)

        @block.scalar
        def _(act):
            count = [0]

            def link(ins):
                count[0] += 1
                ins.then_inc(act_link, 1)
                act.wait_ge(act_link, count[0])

            def hi(n, value=None):
                if n >= NS:
                    return
                if value is None:
                    act.wait_ge(raw_landed[n % RING], landed[n])
                    if n >= RING:
                        act.wait_ge(slab_done, n - RING + 1)
                else:
                    act.wait_ge(raw_landed[n % RING], value[0])
                    act.wait_ge(slab_done, value[1])
                m = slabs[n][2] * slabs[n][3]
                act.activation(whi[:, n % RING, :m], raw[:, n % RING, :m], ACT.Copy).then_inc(hi_ready, 1)

            def loop_hi(i, n):
                hi(n, (i * (landed[n] - landed[n - RING]) + landed[n], i * RING + (n - RING + 1)))

            def empty(n, out, func=ACT.Copy, src=None, **kw):
                act.wait_ge(slab_done, n + 1)
                return act.activation(out, src, func, **kw)

            def tbank(n):
                return tb[:, n % 2, :]

            def sumsq(name, src, quarters=range(4), of=None, counted=None):
                k = NORM[name]
                for q in quarters:
                    if of is not None:
                        wait_quarter(act, of, q)
                    elif name in SRC:
                        act.wait_ge(nrm["src"], src_count(name, q))
                    count = SS[name] + q if counted is None else counted
                    if count:
                        act.wait_ge(nrm["ss"], count)
                    t, c = QUARTERS[q]
                    s = acc[:, c, t, :] if of is not None else quarter(src, q)
                    act.activation(junk[:, :], s, ACT.Square, scale=D ** -0.5, accum_out=ss[:, k, t, c:c + 1]).then_inc(nrm["ss"], 1)

            def fill(name, dst, gain, k0=0, shared=False):
                for count, g, cut in fill_steps(name):
                    act.wait_ge(fil["t"], count)
                    o = fill_bank(name, g).rearrange("p (k t) -> p k t", k=2)
                    for k in range(2):
                        kt = k0 + g * 2 + k
                        c = gain if shared else gain + kt
                        last = act.activation(dst[:, kt, cut], o[:, k, cut], ACT.Copy, scale=cols[:, c:c + 1])
                    last.then_inc(fil["hi"], 1)

            act.dma_start(fs[0:8, 0, 0:P], w["norm_mix_g"].rearrange("a (k p) -> (a k) p", p=P)).then_inc(first_rows_in, 16)
            act.dma_start(fs[8:16, 0, 0:P], w["hgrn_lb_logits"].rearrange("a (k p) -> (a k) p", p=P)).then_inc(first_rows_in, 16)
            act.wait_ge(consts_ready, 1)
            act.activation(small[:, 63:64], half_neg[:, 0:1], ACT.Sigmoid)
            for q in range(4):
                act.wait_ge(x_in[q], 16)
                sumsq("x", h, [q])
            act.wait_ge(cols_ready, 1)
            act.wait_ge(raw_landed[0], landed[0])
            for s, signal in ((slice(0, SLAB // 2), first_half_hi), (slice(SLAB // 2, SLAB), hi_ready)):
                act.activation(whi[:, 0, s], raw[:, 0, s], ACT.Copy).then_inc(signal, 1)
            fill("x", xhi, C["norm_mix_g"])
            for n in range(1, RING):
                hi(n)
            act.wait_ge(lb_ready, 1)
            act.activation(small[:, 52:56], small[:, 48:52], ACT.Sigmoid).then_inc(lb_ready, 1)

            A = first["gf"]
            for j in range(2):
                empty(A + j, dz[:, 0, j * 512:j * 512 + 512], ACT.Sigmoid, tbank(A + j)).then_inc(act_emptied, 1)
                hi(A + j + RING)
            for j in range(2):
                n = first["gq"] + j
                empty(n, dz[:, 1, j * 512:j * 512 + 512], ACT.Sigmoid, tbank(n)).then_inc(hg["sq"], 1)
                hi(n + RING)
                if j == 0:
                    act.wait_ge(mem_in, 16)
                    sumsq("mem", xn)
            act.wait_ge(hg["kk"], 2)
            act.activation(bb[:, :], dz[:, 0, :], ACT.Ln).then_inc(hg["ln"], 1)
            act.wait_ge(fx["z"], 1)
            link(act.activation(am[0:8, 2, :], am[0:8, 0, :], ACT.Exp, scale=-1.0))
            link(act.activation(am[0:8, 3, :], am[0:8, 1, :], ACT.Exp, scale=-1.0))
            act.activation(am[0:8, 2:4, :], am[0:8, 2:4, :], ACT.Ln, bias=1.0).then_inc(fx["l"], 1)
            hi(first["ff"] + RING)
            act.wait_ge(lamx, 1)
            act.activation(rden[:, 3, 0:2], den[:, 3, 0:2], ACT.Exp).then_inc(lam_ready, 1)
            act.wait_ge(cols_ready, 2)
            fill("mem", mhi, C["norm_mem_g"])
            for j in range(2):
                n = first["fq"] + j
                empty(n, fqT[:, 2 * j:2 * j + 2, :], ACT.Copy, tbank(n), scale=0.125).then_inc(act_emptied, 1)
                hi(n + RING)
            for j in range(2):
                n = first["fk"] + j
                empty(n, fkT[:, 2 * j:2 * j + 2, :], ACT.Copy, tbank(n)).then_inc(act_emptied, 1)
                hi(n + RING)
                if j:
                    act.wait_ge(mem2_in, 16)
                    sumsq("mem2", xn)
            for j, (name, dst) in enumerate((("fv", fv), ("gi", gi))):
                n = first[name] + 1
                hi(n - 1 + RING)
                empty(n, dst[:, :, :], ACT.Copy, acc[:, j, :, :]).then_inc(act_emptied, 1)
                hi(n + RING)
            n = first["gg"] + 1
            hi(n - 1 + RING)
            empty(n, gg[:, :, :], ACT.Sigmoid, acc[:, 0, :, :]).then_inc(hg["gsig"], 1)
            hi(n + RING)

            def fox_exp(i):
                act.wait_ge(fox["max"], i + 1)
                s = fs[:, i % 2, :]
                act.activation(s[:, 0:P], s[:, 0:P], ACT.Exp, bias=nmx[:, i % 2, 0:1], accum_out=den[:, i % 2, 0:1])
                act.activation(s[:, P:384], s[:, P:384], ACT.Exp, bias=nmx[:, i % 2, 1:2], accum_out=den[:, i % 2, 1:2])\
                    .then_inc(fox["exp"], 1)

            def fox_copy(i):
                act.wait_ge(fox["pt"], i + 1)
                if i >= 2:
                    act.wait_ge(fox["pv"], i - 1)
                act.activation(fpt[:, i % 2, :], tb[:, 3, 0:384], ACT.Copy).then_inc(fox["ptc"], 1)

            def fox_hi(i):
                p0 = (i % 2) * 64
                act.wait_ge(fox["pv"], i + 1)
                act.activation(xhi[p0:p0 + 64, i // 2, :], tb[p0:p0 + 64, 3, 0:T], ACT.Copy).then_inc(fox["pvhi"], 1)

            def hg_exp(m):
                act.wait_ge(hg["d"], m)
                z = lvl_view(dz[:, m % 2, :], m)
                act.activation(z[:, :, 0, :], z[:, :, 0, :], ACT.Exp, scale=-1.0)
                src = lvl_view(bb[:, :], m) if m == LEVELS - 1 else z
                act.activation(z[:, :, 1, :], src[:, :, 1, :], ACT.Exp).then_inc(hg["e"], 1)

            B = first["xk"]
            hg_exp(1)
            for i in range(12):
                n = B + i
                if n < first["xv"]:
                    empty(n, xkT[:, 2 * i:2 * i + 2, :], ACT.Copy, tbank(n)).then_inc(act_emptied, 1)
                elif n < first["km"]:
                    if i % 2:
                        c = (i - 5) // 2 * 512
                        empty(n, xv[:, :, c:c + 512], ACT.Copy, acc[:, 0, :, :]).then_inc(act_emptied, 1)
                elif n < first["vm"]:
                    j = n - first["km"]
                    empty(n, kmT[:, 2 * j:2 * j + 2, :], ACT.Copy, tbank(n)).then_inc(act_emptied, 1)
                elif i == 11:
                    empty(n, vm[:, :, :], ACT.Copy, acc[:, 0, :, :]).then_inc(act_emptied, 1)
                if i == 8:
                    fox_copy(7)
                hi(n + RING)
                if i < 8:
                    if i:
                        fox_copy(i - 1)
                    if i == 7:
                        fill("mem2", mhi, C["norm_mem_2"])
                        hg_exp(8)
                    fox_exp(i)
                    if 2 <= i + 1 < 8:
                        hg_exp(i + 1)
                    if i:
                        fox_hi(i - 1)
                elif i == 8:
                    fox_hi(7)
                elif i == 9:
                    act.wait_ge(hg["out"], 1)
                    act.activation(dz[:, 1, :], acc[:, 1, :, :], ACT.Square).then_inc(hg["sq2"], 1)
                elif i == 11:
                    fill("rec", xhi, C["hgrn_norm_g"], k0=4, shared=True)

            for j in range(2):
                hi(first["wo"] + j + RING)
            sumsq("h1", h)
            fill("h1", xhi, C["norm_x_g"])
            for j in (2, 3):
                hi(first["wo"] + j + RING)

            def cross_exp(i):
                act.wait_ge(cr["max"], i + 1)
                for t in range(TT):
                    o = cross_bank(i)[:, t * T:t * T + T]
                    last = act.activation(cs[:, i, t * T:t * T + T], o, ACT.Exp, bias=nmx[:, i, t:t + 1], scale=1.0 / 16,
                                          accum_out=den[:, i, t:t + 1])
                last.then_inc(cr["exp"], 1)

            def cross_copy(i):
                act.wait_ge(cr["pt"], i + 1)
                if i >= 2:
                    act.wait_ge(cr["pv"], i - 1)
                act.activation(cpt[:, i % 2, :], cross_pt_bank(i), ACT.Copy).then_inc(cr["ptc"], 1)

            def cross_hi(i):
                act.wait_ge(cr["pv"], i + 1)
                act.activation(chi[:, 2 * i:2 * i + 2, :], cross_bank(i), ACT.Copy).then_inc(cr["pvhi"], 1)

            for j in range(4):
                n = first["xq"] + j
                empty(n, xqT[:, 2 * j:2 * j + 2, :], ACT.Copy, tbank(n)).then_inc(act_emptied, 1)
                hi(n + RING)
                if j == 1:
                    cross_exp(0)
                elif j == 2:
                    cross_copy(0)
                    cross_exp(1)
            cross_hi(0)
            cross_copy(1)
            cross_hi(1)
            cross_exp(2)
            cross_exp(3)
            cross_copy(2)
            cross_copy(3)
            hi(first["xo"] + RING)
            cross_hi(2)
            cross_hi(3)
            hi(first["xo"] + 1 + RING)
            sumsq("h2", h)
            fill("h2", xhi, C["norm_ff_g"])
            for j in (2, 3):
                hi(first["xo"] + j + RING)

            def relu_step(bank, done, j, dst):
                act.wait_ge(slab_done, done)
                act.activation(ru[:, :], tb[:, bank, :], ACT.Relu).then_inc(act_emptied, 1)

            def relu_hi(dst, sq_count):
                act.wait_ge(ffn["sq"], sq_count)
                act.activation(dst, sq[:, :], ACT.Copy).then_inc(ffn["hi"], 1)

            n0 = first["w1"]
            with act.Fori(0, 5) as i:
                for u in range(RING):
                    relu_step(u, i * RING + (n0 + u + 1), None, None)
                    loop_hi(i, n0 + u + RING)
                    relu_hi(hid_hi[:, bass.ds(i * 6 + 2 * u, 2), :], i * RING + (u + 1))
            relu_step(0, n0 + 16, None, None)
            hi(n0 + 15 + RING)
            relu_hi(hid_hi[:, 30:32, :], 16)
            n0 = first["w2"]
            with act.Fori(0, 4) as i:
                for u in range(RING):
                    loop_hi(i, n0 + u + RING)
            for j in range(12, 14):
                hi(n0 + j + RING)
            for q in range(4):
                sumsq("h3", h, [q], counted=SS["h3"] + 2 * q)
                sumsq("x2", xn, [q], counted=SS["h3"] + 2 * q + 1)
            fill("x2", xhi, C["norm_mix_pre_2"])
            for j in (14, 15):
                hi(n0 + j + RING)

            for j in range(4):
                n = first["qd"] + j
                empty(n, qdT[:, 2 * j:2 * j + 2, :], ACT.Copy, tbank(n), scale=0.125).then_inc(act_emptied, 1)
                hi(n + RING)
            for j in range(4):
                n = first["kd"] + j
                empty(n, kdT[:, 2 * j:2 * j + 2, :], ACT.Copy, tbank(n)).then_inc(act_emptied, 1)
                hi(n + RING)
            for j in range(4):
                n = first["vd"] + j
                if j == 3:
                    act.wait_ge(slab_done, n + 1)
                    act.activation(vd[:, 0, :], acc[:, :, 0, :], ACT.Copy)
                    act.activation(vd[:, 1, :], acc[:, :, 1, :], ACT.Copy).then_inc(act_emptied, 1)
                hi(n + RING)

            def diff_exp(i):
                for c in range(2):
                    act.wait_ge(df["max"], 2 * i + c + 1)
                    s = ds_[:, c, :]
                    act.activation(s[:, 0:P], s[:, 0:P], ACT.Exp, bias=nmx[:, c, 0:1], accum_out=den[:, c, 0:1])
                    act.activation(s[:, P:384], s[:, P:384], ACT.Exp, bias=nmx[:, c, 1:2], accum_out=den[:, c, 1:2])\
                        .then_inc(df["exp"], 1)

            def diff_copy(i):
                act.wait_ge(df["pt"], i + 1)
                if i:
                    act.wait_ge(df["pv"], i)
                act.activation(dpt[:, :], acc[:, 0, 0, 0:384], ACT.Copy).then_inc(df["ptc"], 1)

            def diff_out(i):
                act.wait_ge(df["pv"], i + 1)
                for t in range(TT):
                    last = act.activation(xn[:, t, i * P:i * P + P], acc[:, 0, 1, t * P:t * P + P], ACT.Copy, scale=rden[:, 0, t:t + 1])
                last.then_inc(df["o"], 1)

            def mem_exp(i):
                act.wait_ge(me["max"], i + 1)
                for t in range(TT):
                    last = act.activation(ms[:, t * T:t * T + T], acc[:, 1, 0, t * T:t * T + T], ACT.Exp,
                                          bias=nmx[:, 2, t:t + 1], scale=P ** -0.5, accum_out=den[:, 2, t:t + 1])
                last.then_inc(me["exp"], 1)

            def mem_copy(i):
                act.wait_ge(me["pt"], i + 1)
                if i:
                    act.wait_ge(me["pv"], i)
                act.activation(mpt[:, :], acc[:, 1, 1, :], ACT.Copy).then_inc(me["ptc"], 1)

            def mem_hi(i):
                act.wait_ge(me["pv"], i + 1)
                act.activation(ohi[:, i, :], acc[:, 0, 1, 0:T], ACT.Copy).then_inc(me["pvhi"], 1)

            for i in range(16):
                n = first["up"] + i
                if i < 2:
                    dst = upad[:, 2 * i:2 * i + 2, PAD:]
                    empty(n, dst, ACT.Copy, tbank(n).rearrange("p (k t) -> p k t", k=2)).then_inc(act_emptied, 1)
                elif i < 4:
                    empty(n, qmT[:, 2 * i - 4:2 * i - 2, :], ACT.Copy, tbank(n)).then_inc(act_emptied, 1)
                else:
                    empty(n, gates[:, 2 * i - 8:2 * i - 6, :], ACT.Copy if i < 12 else ACT.Sigmoid,
                          tbank(n)).then_inc(act_emptied, 1)
                if 1 <= i <= 8:
                    diff_copy(i - 1)
                if 9 <= i <= 12:
                    mem_copy(i - 9)
                hi(n + RING)
                if i < 8:
                    diff_exp(i)
                if 1 <= i <= 8:
                    diff_out(i - 1)
                if 10 <= i <= 13:
                    mem_hi(i - 10)
                if 8 <= i <= 11:
                    mem_exp(i - 8)
                if i >= 12:
                    s = gates[:, 4 * (i - 12):4 * (i - 11), :]
                    act.wait_ge(act_emptied, act_evacs[first["ga"] + 7])
                    act.activation(s, s, ACT.Sigmoid).then_inc(gates_ready, 1)
                if i == 14:
                    act.wait_ge(pl["mm"], 1)
                    for g in range(4):
                        c = C["pool_scale_2"] + g
                        last = act.activation(phi[:, g, :], acc[:, 0, g // 2, (g % 2) * T:(g % 2) * T + T], ACT.Copy, scale=cols[:, c:c + 1])
                    last.then_inc(pl["hi"], 1)
            hi(first["pb"] + RING)
            fill("a", xhi, C["subln_g_2"], shared=True)
            hi(first["pb"] + 1 + RING)
            for j in range(2):
                hi(first["mb"] + j + RING)

            def mix_hi(j):
                act.wait_ge(mix["f"], j + 1)
                act.activation(yhi[:, 2 * j:2 * j + 2, :], mixf[:, :], ACT.Copy).then_inc(mix["hi"], 1)

            for j in range(4):
                hi(first["ab"] + j + RING)
                mix_hi(j)
            for j in range(2):
                hi(first["w3"] + j + RING)
            sumsq("mix", acc, of=first["w3"] + 3)
            sumsq("h4", h)
            fill("h4", xhi, C["norm_ffn_pre_2"])
            for j in (2, 3):
                hi(first["w3"] + j + RING)

            def conv_base(b, done, j):
                act.wait_ge(slab_done, done)
                for g in range(2):
                    a = C["conv_w_2"] + 2 * 44 + g * NT2
                    c = C["conv_b_2"] + g * NT2
                    last = act.activation(cy[:, b, g, :], tb[:, b, g * T:g * T + T], ACT.Identity,
                                          scale=cols[:, bass.ds(j + a, 1)], bias=cols[:, bass.ds(j + c, 1)])
                last.then_inc(cvs["base"], 1)

            def conv_gelu(b, k):
                act.wait_ge(cvs["y"], k)
                act.activation(cg[:, :], cy[:, b, 0, :], ACT.Gelu_apprx_tanh).then_inc(cvs["gelu"], 1)

            def conv_hi(j, k):
                act.wait_ge(cvs["f"], k)
                act.activation(vhi[:, bass.ds(j, 1), :], cf[:, :], ACT.Copy).then_inc(cvs["hi"], 1)

            n0 = first["cv"]
            act.activation(small[:, 0:1], half_neg[:, 0:1], ACT.Gelu_apprx_tanh)
            conv_base(0, n0 + 1, 0)
            hi(n0 + RING)
            with act.Fori(0, 7) as i:
                for u in range(RING):
                    conv_base((u + 1) % RING, i * RING + (n0 + u + 2), i * RING + (u + 1))
                    conv_gelu(u, i * RING + (u + 1))
                    loop_hi(i, n0 + u + 1 + RING)
                    conv_hi(i * RING + u, i * RING + (u + 1))
            conv_gelu(0, 22)
            conv_hi(21, 22)
            for j in range(NT2 // 2):
                hi(first["wd"] + j + RING)
            sumsq("end", acc, of=NS - 1)
            for q, (t, c) in enumerate(QUARTERS):
                act.wait_ge(nrm["src"], SRC["end"] + q + 1)
                act.dma_start(out[0, t * P:t * P + P, c * 512:c * 512 + 512], quarter(h, q)).then_inc(stored, 16)
            act.wait_ge(stored, 64)

        @block.vector
        def _(dve):
            count = [0]

            def link(ins):
                count[0] += 1
                ins.then_inc(dve_link, 1)
                dve.wait_ge(dve_link, count[0])

            def lo(n, value=None):
                if n >= NS:
                    return
                dve.wait_ge(hi_ready, n + 1 if value is None else value)
                m = slabs[n][2] * slabs[n][3]
                dve.tensor_tensor(wlo[:, n % RING, :m], raw[:, n % RING, :m], whi[:, n % RING, :m].bitcast(F32),
                                  ALU.subtract).then_inc(lo_ready, 1)

            def loop_lo(i, n):
                lo(n, i * RING + (n + 1))

            def fill(name, dst_hi, dst, gain, k0=0, shared=False):
                for count, g, cut in fill_steps(name):
                    dve.wait_ge(fil["hi"], count)
                    o = fill_bank(name, g).rearrange("p (k t) -> p k t", k=2)
                    for k in range(2):
                        kt = k0 + g * 2 + k
                        c = gain if shared else gain + kt
                        last = dve.scalar_tensor_tensor(dst[:, kt, cut], o[:, k, cut], cols[:, c:c + 1],
                                                        dst_hi[:, kt, cut].bitcast(F32), ALU.mult, ALU.subtract)
                    last.then_inc(fil["lo"], 1)

            def tbank(n):
                return tb[:, n % 2, :]

            def residual(n, name):
                for q in range(4):
                    wait_quarter(dve, n, q)
                    t, c = QUARTERS[q]
                    dve.tensor_tensor(quarter(h, q), acc[:, c, t, :], quarter(h, q), ALU.add).then_inc(nrm["src"], 1)
                dve.wait_ge(nrm["src"], SRC[name] + 4)
                dve.sem_inc(dve_emptied, 1)

            dve.wait_ge(consts_ready, 1)
            dve.wait_ge(cols_t, 1)
            dve.tensor_copy(cols[:, 0:16], acc[:, 0, 0, 0:16]).then_inc(cols_ready, 1)
            dve.wait_ge(cols_ready, 1)
            dve.tensor_tensor(small[:, 48:52], cols[:, C["lb"]:C["lb"] + 4], cols[:, C["lb"] + 4:C["lb"] + 8],
                              ALU.subtract).then_inc(lb_ready, 1)
            dve.wait_ge(first_half_hi, 1)
            s = slice(0, SLAB // 2)
            dve.tensor_tensor(wlo[:, 0, s], raw[:, 0, s], whi[:, 0, s].bitcast(F32), ALU.subtract).then_inc(first_half_lo, 1)
            dve.wait_ge(hi_ready, 1)
            s = slice(SLAB // 2, SLAB)
            dve.tensor_tensor(wlo[:, 0, s], raw[:, 0, s], whi[:, 0, s].bitcast(F32), ALU.subtract).then_inc(lo_ready, 1)
            fill("x", xhi, xlo, C["norm_mix_g"])
            for n in range(1, RING):
                lo(n)
            dve.wait_ge(lam_in, 64)
            lam = fpt[:, 0, 0:256].rearrange("p (a b c) -> p a b c", a=2, b=2)
            link(dve.tensor_tensor(fpt[:, 1, 0:128].rearrange("p (a c) -> p a c", a=2), lam[:, :, 0, :], lam[:, :, 1, :],
                                   ALU.mult))
            dve.tensor_reduce(den[:, 3, 0:2], fpt[:, 1, 0:128].rearrange("p (a c) -> p a c", a=2), AX, ALU.add)\
                .then_inc(lamx, 1)
            dve.wait_ge(lb_ready, 2)
            link(dve.tensor_scalar(small[:, 48:52], small[:, 52:56], -1.0, 1.0, ALU.mult, ALU.add))

            A = first["gf"]
            for j in range(2):
                dve.wait_ge(act_emptied, act_evacs[A + j])
                for i in range(2):
                    s = slice(j * 512 + i * T, j * 512 + i * T + T)
                    hd = 2 * j + i
                    last = dve.tensor_scalar(dz[:, 0, s], dz[:, 0, s], small[:, 48 + hd:49 + hd], small[:, 52 + hd:53 + hd],
                                             ALU.mult, ALU.add)
                link(last)
                s = slice(j * 512, j * 512 + 512)
                link(dve.tensor_scalar(kk[:, s], dz[:, 0, s], -1.0, 1.0, ALU.mult, ALU.add))
                dve.tensor_scalar(dz[:, 0, s], dz[:, 0, s], LN_MIN, None, ALU.max).then_inc(hg["kk"], 1)
                lo(A + j + RING)
            for j in range(2):
                n = first["gq"] + j
                dve.wait_ge(hg["sq"], j + 1)
                dve.tensor_tensor(qs[:, j * 512:j * 512 + 512], tbank(n), dz[:, 1, j * 512:j * 512 + 512], ALU.mult)\
                    .then_inc(hg["qs"], 1)
                dve.wait_ge(hg["qs"], j + 1)
                dve.sem_inc(dve_emptied, 1)
                lo(n + RING)
            dve.wait_ge(cols_t, 2)
            dve.tensor_copy(cols[:, 16:NC0 + NCW], acc[:, 0, 1, 16:NC0 + NCW]).then_inc(cols_ready, 1)
            dve.wait_ge(cols_ready, 2)
            dve.tensor_scalar(cols[:, 69:70], cols[:, 69:70], 1.0 - LAM_INIT, None, ALU.mult)
            n = first["ff"]
            dve.wait_ge(slab_done, n + 1)
            dve.wait_ge(bias_in, 16)
            zf, az, mz = (am[0:8, i:i + 2, :].rearrange("p a c -> p (a c)") for i in (6, 0, 4))
            link(dve.tensor_scalar(zf, tb[0:8, n % 2, 0:T], small[0:8, 59:60], None, ALU.add))
            dve.sem_inc(dve_emptied, 1)
            dve.tensor_scalar(mz, zf, 0.0, None, ALU.min)
            dve.scalar_tensor_tensor(az, zf, -1.0, zf, ALU.mult, ALU.max).then_inc(fx["z"], 1)
            dve.memset(dz[:, 1, 0:P], 0.0)
            link(dve.memset(am[0:8, 8:10, :], 0.0))
            dve.wait_ge(hg["ln"], 1)
            for s in range(8):
                last = dve.tensor_tensor_scan(dz[:, 0, s * P:s * P + P], bb[:, s * P:s * P + P], dz[:, 1, 0:P], 0.0,
                                              ALU.add, ALU.add)
            link(last)
            link(dve.tensor_copy(bb[:, :], dz[:, 0, :]))
            lo(first["ff"] + RING)
            dve.wait_ge(fx["l"], 1)
            lf = am[0:8, 2:4, :].rearrange("p a c -> p (a c)")
            link(dve.tensor_tensor(zf, lf, mz, ALU.subtract))
            dve.tensor_tensor_scan(negF[0:8, :], zf, am[0:8, 8:10, :].rearrange("p a c -> p (a c)"), 0.0, ALU.add, ALU.add)\
                .then_inc(fx["F"], 1)
            dve.wait_ge(lam_ready, 1)
            link(dve.tensor_tensor(small[:, 56:57], rden[:, 3, 1:2], rden[:, 3, 0:1], ALU.subtract))
            link(dve.tensor_scalar(small[:, 56:57], small[:, 56:57], -LAM_INIT, None, ALU.add))
            fill("mem", mhi, mlo, C["norm_mem_g"])
            for n in range(first["fq"], first["gg"] + 1):
                lo(n + RING)

            def hg_diff(m):
                if m >= 2:
                    dve.wait_ge(hg["prod"], m - 1)
                z, b = lvl_view(dz[:, m % 2, :], m), lvl_view(bb[:, :], m)
                half = 1 << (m - 1)
                if m == LEVELS - 1:
                    mid = b[:, :, 0, half - 1:half].broadcast_to([P, b.shape[1], half])
                    dve.tensor_tensor(z[:, :, 0, :], b[:, :, 0, :], mid, ALU.subtract).then_inc(hg["d"], 1)
                    return
                b3 = b.rearrange("p g r u -> p g (r u)")
                mid = b3[:, :, half - 1:half].broadcast_to([P, b.shape[1], 2 * half])
                dve.tensor_tensor(z.rearrange("p g r u -> p g (r u)"), b3, mid, ALU.subtract).then_inc(hg["d"], 1)

            hg_diff(1)
            n = first["gg"] + 1
            dve.wait_ge(hg["gsig"], 1)
            dve.tensor_tensor(gg[:, :, :], acc[:, 0, :, :], gg[:, :, :], ALU.mult).then_inc(hg["gg"], 1)
            dve.wait_ge(hg["gg"], 1)
            dve.sem_inc(dve_emptied, 1)
            lo(n + RING)

            def row_max(src, i, scale):
                dve.tensor_reduce(mx[:, i, 0:1], src[:, 0:P], AX, ALU.max)
                link(dve.tensor_reduce(mx[:, i, 1:2], src[:, P:384], AX, ALU.max))
                return dve.tensor_scalar(nmx[:, i, 0:2], mx[:, i, 0:2], -scale, None, ALU.mult)

            def fox_mask(i):
                dve.wait_ge(fox["scores"], i + 1)
                if i == 0:
                    dve.wait_ge(consts_ready, 2)
                if i >= 2:
                    dve.wait_ge(fox["pt"], i - 1)
                s = fs[:, i % 2, :]
                dve.tensor_tensor(s, tb[:, 2, 0:384], causal[:, :], ALU.add).then_inc(fox["read"], 1)
                dve.wait_ge(fox["read"], i + 1)
                row_max(s, i % 2, 1.0).then_inc(fox["max"], 1)

            def fox_norm(i):
                dve.wait_ge(fox["exp"], i + 1)
                link(dve.reciprocal(rden[:, i % 2, 0:2], den[:, i % 2, 0:2]))
                s = fs[:, i % 2, :]
                dve.tensor_scalar(s[:, 0:P], s[:, 0:P], rden[:, i % 2, 0:1], None, ALU.mult)
                dve.tensor_scalar(s[:, P:384], s[:, P:384], rden[:, i % 2, 1:2], None, ALU.mult).then_inc(fox["p"], 1)

            def fox_lo(i):
                p0 = (i % 2) * 64
                dve.wait_ge(fox["pvhi"], i + 1)
                dve.tensor_tensor(xlo[p0:p0 + 64, i // 2, :], tb[p0:p0 + 64, 3, 0:T],
                                  xhi[p0:p0 + 64, i // 2, :].bitcast(F32), ALU.subtract).then_inc(fox["pvlo"], 1)

            def hg_merge(m):
                dve.wait_ge(hg["prod"], m + 1)
                if m:
                    dve.wait_ge(hg["merged"], m)
                if m == LEVELS - 1:
                    dve.tensor_copy(am[:, 8:12, :], acc[:, 1, 0, :].rearrange("p (h t) -> p h t", h=4))\
                        .then_inc(hg["merged"], 1)
                    return
                for t in range(TT):
                    o = acc[:, 1, t, :].rearrange("p (h t) -> p h t", h=4)
                    dst = am[:, 4 * t:4 * t + 4, :]
                    if m == 0:
                        eye = ident[:, :].rearrange("p (a t) -> p a t", a=1).broadcast_to([P, 4, P])
                        last = dve.tensor_tensor(dst, o, eye, ALU.mult)
                    else:
                        half = 1 << (m - 1)
                        mask = lvl[:, m - 1, :].bitcast(U32).rearrange("p (a g r u) -> p a g r u", a=1, r=2, u=half)[:, :, :, 1, :]
                        mask = mask.broadcast_to([P, 4, 64 // half, half])
                        dst = dst.rearrange("p h (g r u) -> p h g r u", r=2, u=half)[:, :, :, 1, :]
                        last = dve.copy_predicated(dst, mask, acc[:, 1, t, 0:256].rearrange("p (h g u) -> p h g u", h=4, u=half))
                last.then_inc(hg["merged"], 1)

            B = first["xk"]
            for i in range(12):
                lo(B + i + RING)
                if i == 7:
                    fill("mem2", mhi, mlo, C["norm_mem_2"])
                    hg_diff(8)
                if i < 8:
                    fox_mask(i)
                    if 2 <= i + 1 < 8:
                        hg_diff(i + 1)
                    fox_norm(i)
                    hg_merge(i)
                    if i:
                        fox_lo(i - 1)
                elif i == 8:
                    hg_merge(8)
                    fox_lo(7)
                elif i == 9:
                    dve.wait_ge(hg["sq2"], 1)
                    dve.tensor_reduce(small[:, 0:8], dz[:, 1, :].rearrange("p (g v) -> p g v", v=P), AX, ALU.add)\
                        .then_inc(hg["ss"], 1)
                    dve.wait_ge(hg["rs"], 1)
                    for t in range(TT):
                        r = small[:, 8 + 4 * t:12 + 4 * t].rearrange("p (h a) -> p h a", a=1).broadcast_to([P, 4, P])
                        last = dve.tensor_tensor(dz[:, 1, t * 512:t * 512 + 512].rearrange("p (h v) -> p h v", h=4),
                                                 acc[:, 1, t, :].rearrange("p (h v) -> p h v", h=4), r, ALU.mult)
                    last.then_inc(hg["rd"], 1)
                    dve.wait_ge(hg["rd"], 1)
                    dve.tensor_tensor(dz[:, 1, :], dz[:, 1, :], gg[:, :, :].rearrange("p t c -> p (t c)"), ALU.mult)\
                        .then_inc(hg["rec"], 1)
                elif i == 11:
                    fill("rec", xhi, xlo, C["hgrn_norm_g"], k0=4, shared=True)

            for j in range(2):
                lo(first["wo"] + j + RING)
            residual(first["wo"] + 3, "h1")
            fill("h1", xhi, xlo, C["norm_x_g"])
            for j in (2, 3):
                lo(first["wo"] + j + RING)

            def cross_max(i):
                dve.wait_ge(cr["scores"], i + 1)
                src = cross_bank(i).rearrange("p (t m) -> p t m", t=2)
                link(dve.tensor_reduce(mx[:, i, 0:2], src, AX, ALU.max))
                dve.tensor_scalar(nmx[:, i, 0:2], mx[:, i, 0:2], -1.0 / 16, None, ALU.mult).then_inc(cr["max"], 1)

            def cross_norm(i):
                dve.wait_ge(cr["exp"], i + 1)
                link(dve.reciprocal(rden[:, i, 0:2], den[:, i, 0:2]))
                for t in range(TT):
                    last = dve.tensor_scalar(cs[:, i, t * T:t * T + T], cs[:, i, t * T:t * T + T], rden[:, i, t:t + 1], None,
                                             ALU.mult)
                last.then_inc(cr["p"], 1)

            def cross_lo(i):
                dve.wait_ge(cr["pvhi"], i + 1)
                dve.tensor_tensor(clo[:, 2 * i:2 * i + 2, :], cross_bank(i), chi[:, 2 * i:2 * i + 2, :].bitcast(F32),
                                  ALU.subtract).then_inc(cr["pvlo"], 1)

            for j in range(4):
                if j >= 2:
                    cross_norm(j - 2)
                lo(first["xq"] + j + RING)
                if j in (1, 2):
                    cross_max(j - 1)
            cross_lo(0)
            cross_max(2)
            cross_lo(1)
            cross_max(3)
            cross_norm(2)
            cross_norm(3)
            lo(first["xo"] + RING)
            cross_lo(2)
            cross_lo(3)
            lo(first["xo"] + 1 + RING)
            residual(first["xo"] + 3, "h2")
            fill("h2", xhi, xlo, C["norm_ff_g"])
            for j in (2, 3):
                lo(first["xo"] + j + RING)

            def square(emptied):
                dve.wait_ge(act_emptied, emptied)
                dve.tensor_tensor(sq[:, :], ru[:, :], ru[:, :], ALU.mult).then_inc(ffn["sq"], 1)

            def square_lo(dst, src_hi, k):
                dve.wait_ge(ffn["hi"], k)
                dve.tensor_tensor(dst, sq[:, :], src_hi.bitcast(F32), ALU.subtract).then_inc(ffn["lo"], 1)
                dve.wait_ge(ffn["lo"], k)

            n0 = first["w1"]
            with dve.Fori(0, 5) as i:
                for u in range(RING):
                    square(i * RING + act_evacs[n0 + u])
                    loop_lo(i, n0 + u + RING)
                    s = bass.ds(i * 6 + 2 * u, 2)
                    square_lo(hid_lo[:, s, :], hid_hi[:, s, :], i * RING + (u + 1))
            square(act_evacs[n0 + 15])
            lo(n0 + 15 + RING)
            square_lo(hid_lo[:, 30:32, :], hid_hi[:, 30:32, :], 16)
            n0 = first["w2"]
            with dve.Fori(0, 4) as i:
                for u in range(RING):
                    loop_lo(i, n0 + u + RING)
            for j in range(12, 14):
                lo(n0 + j + RING)
            dve.wait_ge(gfin_in, 16)
            for q in range(4):
                wait_quarter(dve, n0 + 15, q)
                t, c = QUARTERS[q]
                dve.tensor_tensor(quarter(h, q), acc[:, c, t, :], quarter(h, q), ALU.add).then_inc(nrm["src"], 1)
                dve.wait_ge(nrm["src"], SRC["h3"] + 2 * q + 1)
                dve.tensor_tensor(quarter(xn, q), quarter(h, q), gbc[:, c * 512:c * 512 + 512], ALU.mult).then_inc(nrm["src"], 1)
            dve.sem_inc(dve_emptied, 1)
            fill("x2", xhi, xlo, C["norm_mix_pre_2"])
            for j in (14, 15):
                lo(n0 + j + RING)
            for t in range(TT):
                last = dve.tensor_scalar(h[:, t, :], xn[:, t, :], rs[:, NORM["h3"], t:t + 1], None, ALU.mult)
            last.then_inc(h_ready, 1)

            for n in range(first["qd"], first["up"]):
                lo(n + RING)

            def diff_mask(i):
                for c in range(2):
                    if c == 0:
                        dve.wait_ge(df["scores"], i + 1)
                        if i:
                            dve.wait_ge(df["pt"], i)
                        else:
                            dve.wait_ge(consts_ready, 3)
                    s = ds_[:, c, :]
                    dve.scalar_tensor_tensor(s, ndist[:, :], ALIBI[i], tb[:, 2 + c, 0:384], ALU.mult, ALU.add)\
                        .then_inc(df["read"], 1)
                    dve.wait_ge(df["read"], 2 * i + c + 1)
                    row_max(s, c, 1.0).then_inc(df["max"], 1)

            def diff_combine(i):
                dve.wait_ge(df["exp"], 2 * i + 2)
                dve.reciprocal(rden[:, 1, 0:2], den[:, 1, 0:2])
                link(dve.tensor_scalar(rden[:, 2, 0:2], den[:, 0, 0:2], small[:, 56:57], None, ALU.mult))
                link(dve.tensor_tensor(rden[:, 1, 0:2], rden[:, 1, 0:2], rden[:, 2, 0:2], ALU.mult))
                if i:
                    dve.wait_ge(df["o"], i)
                dve.reciprocal(rden[:, 0, 0:2], den[:, 0, 0:2])
                s0, s1 = ds_[:, 0, :], ds_[:, 1, :]
                dve.scalar_tensor_tensor(s0[:, 0:P], s1[:, 0:P], rden[:, 1, 0:1], s0[:, 0:P], ALU.mult, ALU.add)
                dve.scalar_tensor_tensor(s0[:, P:384], s1[:, P:384], rden[:, 1, 1:2], s0[:, P:384], ALU.mult, ALU.add)\
                    .then_inc(df["p"], 1)

            def mem_max(i):
                dve.wait_ge(me["scores"], i + 1)
                src = acc[:, 1, 0, :].rearrange("p (t m) -> p t m", t=2)
                link(dve.tensor_reduce(mx[:, 2, 0:2], src, AX, ALU.max))
                dve.tensor_scalar(nmx[:, 2, 0:2], mx[:, 2, 0:2], -(P ** -0.5), None, ALU.mult).then_inc(me["max"], 1)

            def mem_norm(i):
                dve.wait_ge(me["exp"], i + 1)
                link(dve.reciprocal(rden[:, 2, 0:2], den[:, 2, 0:2]))
                for t in range(TT):
                    last = dve.tensor_scalar(ms[:, t * T:t * T + T], ms[:, t * T:t * T + T], rden[:, 2, t:t + 1], None, ALU.mult)
                last.then_inc(me["p"], 1)

            def mem_lo(i):
                dve.wait_ge(me["pvhi"], i + 1)
                dve.tensor_tensor(olo[:, i, :], acc[:, 0, 1, 0:T], ohi[:, i, :].bitcast(F32), ALU.subtract)\
                    .then_inc(me["pvlo"], 1)

            o16 = xn[:, :, :].rearrange("p t (h e) -> p t h e", h=8)
            for i in range(16):
                if 1 <= i <= 8:
                    lo(first["up"] + i - 1 + RING)
                if i < 8:
                    diff_mask(i)
                if 8 <= i <= 11:
                    mem_max(i - 8)
                if i >= 8:
                    lo(first["up"] + i + RING)
                if i < 8:
                    diff_combine(i)
                if 10 <= i <= 13:
                    mem_lo(i - 10)
                if 8 <= i <= 11:
                    mem_norm(i - 8)
                if i == 9:
                    dve.wait_ge(df["o"], 8)
                    sqv = qdT[:, :, :].rearrange("p k t -> p (k t)")
                    link(dve.tensor_tensor(sqv, xn[:, :, :].rearrange("p t c -> p (t c)"),
                                           xn[:, :, :].rearrange("p t c -> p (t c)"), ALU.mult))
                    dve.tensor_reduce(small[:, 16:32], sqv.rearrange("p (g e) -> p g e", e=P), AX, ALU.add).then_inc(oss, 1)
                if i == 10:
                    dve.wait_ge(ors, 1)
                    for t in range(TT):
                        r = small[:, 32 + 8 * t:40 + 8 * t].rearrange("p (h a) -> p h a", a=1).broadcast_to([P, 8, P])
                        last = dve.tensor_tensor(o16[:, t], o16[:, t], r, ALU.mult)
                    last.then_inc(gx, 1)
                if i == 14:
                    dve.wait_ge(pl["hi"], 1)
                    for g in range(4):
                        c = C["pool_scale_2"] + g
                        last = dve.scalar_tensor_tensor(plo[:, g, :], acc[:, 0, g // 2, (g % 2) * T:(g % 2) * T + T], cols[:, c:c + 1],
                                                        phi[:, g, :].bitcast(F32), ALU.mult, ALU.subtract)
                    last.then_inc(pl["lo"], 1)

            gt = gates[:, :, :].rearrange("p k t -> p (k t)")

            def times_gate(n, bank, g, width):
                dve.wait_ge(slab_done, n + 1)
                dve.wait_ge(gates_ready, 4)
                s = slice(g * T, g * T + width)
                src = tb[:, bank:bank + width // 512, :].rearrange("p b c -> p (b c)")
                link(dve.tensor_tensor(gt[:, s], src, gt[:, s], ALU.mult))
                dve.sem_inc(dve_emptied, 1)

            times_gate(first["pb"], 2, 8, 1024)
            lo(first["pb"] + RING)
            times_gate(first["pb"] + 1, 0, 12, 1024)
            fill("a", xhi, xlo, C["subln_g_2"], shared=True)
            lo(first["pb"] + 1 + RING)
            for j in range(2):
                times_gate(first["mb"] + j, 2 * j, 16 + 4 * j, 1024)
                lo(first["mb"] + j + RING)
                a, b = slice((8 + 4 * j) * T, (12 + 4 * j) * T), slice((16 + 4 * j) * T, (20 + 4 * j) * T)
                link(dve.tensor_tensor(gt[:, a], gt[:, a], gt[:, b], ALU.add))
            for j in range(4):
                times_gate(first["ab"] + j, j % 2, 2 * j, 512)
                a, b = slice(2 * j * T, (2 * j + 2) * T), slice((8 + 2 * j) * T, (10 + 2 * j) * T)
                dve.tensor_tensor(mixf[:, :], gt[:, a], gt[:, b], ALU.add).then_inc(mix["f"], 1)
                lo(first["ab"] + j + RING)
                dve.wait_ge(mix["hi"], j + 1)
                dve.tensor_tensor(ylo[:, 2 * j:2 * j + 2, :], mixf[:, :].rearrange("p (k t) -> p k t", k=2),
                                  yhi[:, 2 * j:2 * j + 2, :].bitcast(F32), ALU.subtract).then_inc(mix["lo"], 1)
            for j in range(2):
                lo(first["w3"] + j + RING)

            def post_norm(name, to, gain_in):
                k, made = NORM[name], 4 if name == "end" else 0

                def gained(q):
                    dve.wait_ge(nrm["ss"], SS[name] + q + 1)
                    t, c = QUARTERS[q]
                    dve.tensor_tensor(quarter(xn, q), acc[:, c, t, :], gpost[:, c * 512:c * 512 + 512], ALU.mult)\
                        .then_inc(post_made, 1)

                def added(t):
                    dve.wait_ge(nrm["rs"], RS[name] + t + 1)
                    for q in (2 * t, 2 * t + 1):
                        dve.wait_ge(post_made, made + q + 1)
                        dve.scalar_tensor_tensor(quarter(h, q), quarter(xn, q), rs[:, k, t:t + 1], quarter(h, q), ALU.mult, ALU.add)\
                            .then_inc(nrm["src"], 1)

                dve.wait_ge(gain_in, 16)
                for q in range(3):
                    gained(q)
                added(0)
                gained(3)
                dve.wait_ge(post_made, made + 4)
                dve.sem_inc(dve_emptied, 1)
                added(1)

            dve.wait_ge(fil["t"], FILL["a"][0] + 4)
            dve.wait_ge(h_ready, 1)
            post_norm("mix", "h4", gpost_in)
            fill("h4", xhi, xlo, C["norm_ffn_pre_2"])
            for j in (2, 3):
                lo(first["w3"] + j + RING)

            n0 = first["cv"]

            def conv_taps(b, j, k):
                dve.wait_ge(cvs["base"], k)
                for g in range(2):
                    c = C["conv_w_2"] + 44 + g * NT2
                    last = dve.scalar_tensor_tensor(cy[:, b, g, 1:], tb[:, b, g * T:g * T + T - 1],
                                                    cols[:, bass.ds(j + c, 1)], cy[:, b, g, 1:], ALU.mult, ALU.add)
                last.then_inc(cvs["tap1"], 1)
                dve.wait_ge(cvs["tap1"], k)
                for g in range(2):
                    c = C["conv_w_2"] + g * NT2
                    last = dve.scalar_tensor_tensor(cy[:, b, g, 2:], tb[:, b, g * T:g * T + T - 2],
                                                    cols[:, bass.ds(j + c, 1)], cy[:, b, g, 2:], ALU.mult, ALU.add)
                last.then_inc(cvs["y"], 1)

            def conv_product(b, k):
                dve.wait_ge(cvs["gelu"], k)
                dve.tensor_tensor(cf[:, :], cg[:, :], cy[:, b, 1, :], ALU.mult).then_inc(cvs["f"], 1)

            def conv_lo(j, k):
                dve.wait_ge(cvs["hi"], k)
                s = bass.ds(j, 1)
                dve.tensor_tensor(vlo[:, s, :], cf[:, :].rearrange("p (a t) -> p a t", a=1), vhi[:, s, :].bitcast(F32),
                                  ALU.subtract).then_inc(cvs["lo"], 1)
                dve.wait_ge(cvs["lo"], k)

            conv_taps(0, 0, 1)
            dve.wait_ge(cvs["y"], 1)
            dve.sem_inc(dve_emptied, 1)
            lo(n0 + RING)
            with dve.Fori(0, 7) as i:
                for u in range(RING):
                    conv_taps((u + 1) % RING, i * RING + (u + 1), i * RING + (u + 2))
                    conv_product(u, i * RING + (u + 1))
                    dve.wait_ge(cvs["y"], i * RING + (u + 2))
                    dve.sem_inc(dve_emptied, 1)
                    loop_lo(i, n0 + u + 1 + RING)
                    conv_lo(i * RING + u, i * RING + (u + 1))
            conv_product(0, 22)
            conv_lo(21, 22)
            for j in range(NT2 // 2):
                lo(first["wd"] + j + RING)
            post_norm("end", "end", gpost2_in)


NAMES = ["x", "mem", "norm_mix_g", "w_in", "fox_f_bias", "hgrn_lb_logits", "hgrn_norm_g", "w_out", "norm_x_g",
         "norm_mem_g", "w_xq", "w_xkv", "w_xo", "norm_ff_g", "w1", "w2", "final_norm_g", "mem_2", "norm_mix_pre_2",
         "w_in_2", "lambda_q1_2", "lambda_k1_2", "lambda_q2_2", "lambda_k2_2", "subln_g_2", "w_attn_branch_2",
         "pool_w_2", "pool_scale_2", "w_pool_branch_2", "norm_mem_2", "w_mem_kv_2", "w_mem_branch_2", "w_out_2",
         "norm_mix_post_2", "norm_ffn_pre_2", "w_up_2", "conv_w_2", "conv_b_2", "w_down_2", "norm_ffn_post_2"]


def kernel(**inputs):
    import numpy as np
    import concourse.bacc as bacc
    from concourse import mybir as _mybir
    from concourse.bass_utils import run_bass_kernel_spmd

    nc = bacc.Bacc("TRN2", target_bir_lowering=False, num_devices=1)
    arrays, w = {}, {}
    for name in NAMES:
        a = np.ascontiguousarray(inputs[name])
        arrays[f"in_{name}"] = a
        w[name] = nc.dram_tensor(f"in_{name}", a.shape, _mybir.dt.from_np(a.dtype), kind="ExternalInput").ap()
    out = nc.dram_tensor("out_0", (1, T, D), _mybir.dt.float32, kind="ExternalOutput").ap()
    two_blocks(nc, w, out)
    return run_bass_kernel_spmd(nc, [arrays], core_ids=[0]).results[0]["out_0"]
```
